# Optimizing a Trainium2 kernel written in Bass

```python
import math
import jax, jax.numpy as jnp
from jax import lax
import numpy as np

D_MODEL = 1024
BATCH = 1
SEQ = 256
DEPTH = 2

CHUNK = 64
Q_BLOCK = 128
NORM_EPS = 1e-6
RWKV_HEADS = 8
RWKV_HEAD_DIM = 64
RWKV_WIDTH = RWKV_HEADS * RWKV_HEAD_DIM
DECAY_LORA = 64
ICLR_LORA = 64
GATE_LORA = 128
DECAY_SCALE = math.exp(-0.5)
LNX_EPS = 64e-5
MLA_HEADS = 8
Q_LORA = 384
KV_LORA = 256
QK_NOPE = 64
QK_ROPE = 32
V_HEAD = 64
ROPE_THETA = 10000.0
D_FF = 2816
N_EXPERTS = 8
TOP_K = 2
D_FF_EXPERT = 3584
N_DENSE = (DEPTH + 1) // 2
N_MOE = DEPTH // 2
SHIFT_SIZES = (RWKV_WIDTH, RWKV_WIDTH, RWKV_WIDTH, DECAY_LORA, ICLR_LORA, GATE_LORA)
REST_SIZES = (Q_LORA, KV_LORA, QK_ROPE, D_MODEL, D_MODEL)
SHIFT_WIDTH = sum(SHIFT_SIZES)
IN_WIDTH = SHIFT_WIDTH + sum(REST_SIZES)


def _split(x, sizes):
    out, o = [], 0
    for s in sizes:
        out.append(x[..., o:o + s])
        o += s
    return out

def rmsnorm(x, g):
    xf = x.astype(jnp.float32)
    y = xf * lax.rsqrt(jnp.mean(xf * xf, axis=-1, keepdims=True) + NORM_EPS)
    return (y * g.astype(jnp.float32)).astype(x.dtype)

def ada_modulation(c, w, b):
    mod = jax.nn.silu(c) @ w + b
    shift, scale, gate = jnp.split(mod, 3, axis=-1)
    return shift[:, None, :], scale[:, None, :], gate[:, None, :]

def token_shift(p):
    return jnp.pad(p, ((0, 0), (1, 0), (0, 0)))[:, :-1]

def apply_rope(x, cos, sin):
    x1, x2 = jnp.split(x, 2, axis=-1)
    return jnp.concatenate([x1 * cos - x2 * sin, x1 * sin + x2 * cos], axis=-1)

def _rwkv7_step(state, inp):
    r, w, k, v, a, b = inp
    sa = jnp.einsum('bhvk,bhk->bhv', state, a)
    state = state * w[:, :, None, :] + sa[..., None] * b[:, :, None, :] + v[..., None] * k[:, :, None, :]
    y = jnp.einsum('bhvk,bhk->bhv', state, r)
    return state, y

def rwkv7_branch(p_r, p_k, p_v, p_w, p_a, p_g, w0, w_up, a0, a_up, g_up, k_k, k_a, r_k, lnx_g, lnx_b, w_out):
    dt = p_r.dtype
    B, S, _ = p_r.shape
    H, N = RWKV_HEADS, RWKV_HEAD_DIM
    f = lambda t: t.astype(jnp.float32)
    decay = jnp.exp(-DECAY_SCALE * jax.nn.sigmoid(f(w0) + jnp.tanh(f(p_w)) @ f(w_up)))
    iclr = jax.nn.sigmoid(f(a0) + f(p_a) @ f(a_up))
    gate = jax.nn.sigmoid(f(p_g)) @ f(g_up)
    k = f(p_k)
    kk = (k * f(k_k)).reshape(B, S, H, N)
    kk = kk * lax.rsqrt(jnp.sum(kk * kk, axis=-1, keepdims=True) + 1e-12)
    k = k * (1.0 + (iclr - 1.0) * f(k_a))
    heads = lambda t: t.reshape(B, S, H, N)
    r, k, v, decay, iclr = heads(f(p_r)), heads(k), heads(f(p_v)), heads(decay), heads(iclr)
    a_vec = -kk
    b_vec = kk * iclr
    xs = tuple(jnp.swapaxes(t, 0, 1) for t in (r, decay, k, v, a_vec, b_vec))
    state0 = jnp.zeros((B, H, N, N), jnp.float32)
    _, y = lax.scan(_rwkv7_step, state0, xs)
    y = jnp.swapaxes(y, 0, 1)
    mu = jnp.mean(y, axis=-1, keepdims=True)
    var = jnp.mean(jnp.square(y - mu), axis=-1, keepdims=True)
    y = ((y - mu) * lax.rsqrt(var + LNX_EPS)).reshape(B, S, H * N) * f(lnx_g) + f(lnx_b)
    bonus = jnp.sum(r * k * f(r_k), axis=-1, keepdims=True) * v
    y = (y + bonus.reshape(B, S, H * N)) * gate
    return y.astype(dt) @ w_out

def mla_branch(q_a, kv_a, k_rope, cos, sin, q_norm, w_qb, kv_norm, w_kvb, w_out):
    B, S, _ = q_a.shape
    H = MLA_HEADS
    q = (rmsnorm(q_a, q_norm) @ w_qb).reshape(B, S, H, QK_NOPE + QK_ROPE)
    q_nope, q_pe = q[..., :QK_NOPE], q[..., QK_NOPE:]
    q_pe = apply_rope(q_pe, cos[:, :, None, :], sin[:, :, None, :])
    kv = (rmsnorm(kv_a, kv_norm) @ w_kvb).reshape(B, S, H, QK_NOPE + V_HEAD)
    k_nope, v = kv[..., :QK_NOPE], kv[..., QK_NOPE:]
    k_pe = apply_rope(k_rope, cos, sin)
    q = jnp.concatenate([q_nope, q_pe], axis=-1)
    k = jnp.concatenate([k_nope, jnp.broadcast_to(k_pe[:, :, None, :], (B, S, H, QK_ROPE))], axis=-1)
    scale = (QK_NOPE + QK_ROPE) ** -0.5
    outs = []
    for i in range(S // Q_BLOCK):
        q_lo = i * Q_BLOCK
        k_hi = q_lo + Q_BLOCK
        s = jnp.einsum('bqhd,bkhd->bhqk', q[:, q_lo:k_hi], k[:, :k_hi]).astype(jnp.float32) * scale
        q_chunk = (q_lo + jnp.arange(Q_BLOCK)) // CHUNK
        k_chunk = jnp.arange(k_hi) // CHUNK
        mask = k_chunk[None, :] <= q_chunk[:, None]
        s = jnp.where(mask, s, jnp.finfo(jnp.float32).min)
        p = jax.nn.softmax(s, axis=-1).astype(v.dtype)
        outs.append(jnp.einsum('bhqk,bkhd->bqhd', p, v[:, :k_hi]))
    o = jnp.concatenate(outs, axis=1).reshape(B, S, H * V_HEAD)
    return o @ w_out

def swiglu(h, w1, w3, w2):
    return (jax.nn.silu(h @ w1) * (h @ w3)) @ w2

def moe_swiglu(h, router_w, router_b, w1, w3, w2):
    logits = (h @ router_w).astype(jnp.float32) + router_b.astype(jnp.float32)
    top_v, top_i = lax.top_k(logits, TOP_K)
    probs = jax.nn.softmax(top_v, axis=-1)
    combine = jnp.sum(jax.nn.one_hot(top_i, N_EXPERTS, dtype=jnp.float32) * probs[..., None], axis=-2)
    out = jnp.zeros_like(h)
    for e in range(N_EXPERTS):
        out = out + combine[..., e:e + 1].astype(h.dtype) * swiglu(h, w1[e], w3[e], w2[e])
    return out

def first_inputs(seed: int = 0) -> dict:
    key = jax.random.key(seed)
    keys = iter(jax.random.split(key, 48))
    def nrm(shape, s):
        return s * jax.random.normal(next(keys), shape, jnp.float32)
    L = DEPTH
    RW = RWKV_WIDTH
    x = nrm((BATCH, SEQ, D_MODEL), 1.0)
    c = nrm((BATCH, D_MODEL), 1.0)
    offs = jax.random.randint(next(keys), (BATCH, 1), 0, 4096, dtype=jnp.int32)
    positions = offs + jnp.arange(SEQ, dtype=jnp.int32)[None, :]
    return {
        'x': x,
        'c': c,
        'positions': positions,
        'ada_w': nrm((L, 2, D_MODEL, 3 * D_MODEL), 0.5 * D_MODEL ** -0.5),
        'ada_b': nrm((L, 2, 3 * D_MODEL), 0.02),
        'norm_mix': 1.0 + nrm((L, D_MODEL), 0.05),
        'norm_ffn': 1.0 + nrm((L, D_MODEL), 0.05),
        'norm_final': 1.0 + nrm((D_MODEL,), 0.05),
        'w_in': nrm((L, D_MODEL, IN_WIDTH), D_MODEL ** -0.5),
        'tshift_mu': jax.random.uniform(next(keys), (L, SHIFT_WIDTH), jnp.float32),
        'w0': nrm((L, RW), 0.5),
        'w_up': nrm((L, DECAY_LORA, RW), 0.5 * DECAY_LORA ** -0.5),
        'a0': nrm((L, RW), 0.1),
        'a_up': nrm((L, ICLR_LORA, RW), 0.5 * ICLR_LORA ** -0.5),
        'g_up': nrm((L, GATE_LORA, RW), GATE_LORA ** -0.5),
        'k_k': 0.85 + nrm((L, RW), 0.05),
        'k_a': 1.0 + nrm((L, RW), 0.05),
        'r_k': nrm((L, RWKV_HEADS, RWKV_HEAD_DIM), 0.1),
        'lnx_g': 1.0 + nrm((L, RW), 0.05),
        'lnx_b': nrm((L, RW), 0.02),
        'rwkv_out': nrm((L, RW, D_MODEL), RW ** -0.5),
        'q_norm': 1.0 + nrm((L, Q_LORA), 0.05),
        'w_qb': nrm((L, Q_LORA, MLA_HEADS * (QK_NOPE + QK_ROPE)), Q_LORA ** -0.5),
        'kv_norm': 1.0 + nrm((L, KV_LORA), 0.05),
        'w_kvb': nrm((L, KV_LORA, MLA_HEADS * (QK_NOPE + V_HEAD)), KV_LORA ** -0.5),
        'mla_out': nrm((L, MLA_HEADS * V_HEAD, D_MODEL), (MLA_HEADS * V_HEAD) ** -0.5),
        'w_o': nrm((L, D_MODEL, D_MODEL), D_MODEL ** -0.5),
        'ffn_w1': nrm((N_DENSE, D_MODEL, D_FF), D_MODEL ** -0.5),
        'ffn_w3': nrm((N_DENSE, D_MODEL, D_FF), D_MODEL ** -0.5),
        'ffn_w2': nrm((N_DENSE, D_FF, D_MODEL), D_FF ** -0.5),
        'router_w': nrm((N_MOE, D_MODEL, N_EXPERTS), D_MODEL ** -0.5),
        'router_b': nrm((N_MOE, N_EXPERTS), 0.01),
        'moe_w1': nrm((N_MOE, N_EXPERTS, D_MODEL, D_FF_EXPERT), D_MODEL ** -0.5),
        'moe_w3': nrm((N_MOE, N_EXPERTS, D_MODEL, D_FF_EXPERT), D_MODEL ** -0.5),
        'moe_w2': nrm((N_MOE, N_EXPERTS, D_FF_EXPERT, D_MODEL), D_FF_EXPERT ** -0.5),
    }

def first_block(x, c, positions, ada_w, ada_b, norm_mix, norm_ffn, norm_final, w_in, tshift_mu,
              w0, w_up, a0, a_up, g_up, k_k, k_a, r_k, lnx_g, lnx_b, rwkv_out,
              q_norm, w_qb, kv_norm, w_kvb, mla_out, w_o,
              ffn_w1, ffn_w3, ffn_w2, router_w, router_b, moe_w1, moe_w3, moe_w2):
    inv_freq = ROPE_THETA ** (-jnp.arange(0, QK_ROPE, 2, dtype=jnp.float32) / QK_ROPE)
    ang = positions.astype(jnp.float32)[..., None] * inv_freq
    cos = jnp.cos(ang).astype(x.dtype)
    sin = jnp.sin(ang).astype(x.dtype)
    for l in range(DEPTH):
        shift, scale, gate = ada_modulation(c, ada_w[l, 0], ada_b[l, 0])
        h = rmsnorm(x, norm_mix[l]) * (1.0 + scale) + shift
        proj = h @ w_in[l]
        ps = proj[..., :SHIFT_WIDTH]
        ps = ps + (token_shift(ps) - ps) * tshift_mu[l]
        p_r, p_k, p_v, p_w, p_a, p_g = _split(ps, SHIFT_SIZES)
        q_a, kv_a, k_rope, g_a, g_b = _split(proj[..., SHIFT_WIDTH:], REST_SIZES)
        y_a = rwkv7_branch(p_r, p_k, p_v, p_w, p_a, p_g, w0[l], w_up[l], a0[l], a_up[l], g_up[l],
                           k_k[l], k_a[l], r_k[l], lnx_g[l], lnx_b[l], rwkv_out[l])
        y_b = mla_branch(q_a, kv_a, k_rope, cos, sin, q_norm[l], w_qb[l], kv_norm[l], w_kvb[l], mla_out[l])
        merged = jax.nn.sigmoid(g_a) * y_a + jax.nn.sigmoid(g_b) * y_b
        x = x + gate * (merged @ w_o[l])
        shift, scale, gate = ada_modulation(c, ada_w[l, 1], ada_b[l, 1])
        h = rmsnorm(x, norm_ffn[l]) * (1.0 + scale) + shift
        if l % 2 == 0:
            f = swiglu(h, ffn_w1[l // 2], ffn_w3[l // 2], ffn_w2[l // 2])
        else:
            f = moe_swiglu(h, router_w[l // 2], router_b[l // 2], moe_w1[l // 2], moe_w3[l // 2], moe_w2[l // 2])
        x = x + gate * f
    return rmsnorm(x, norm_final)


DEPTH_2 = 1

GRID_W = 64
CTX_LEN = 256

D_HY = D_MODEL // 4
D_HG = D_MODEL // 2
D_FN = D_MODEL // 4
D_MIX = D_HY + D_HG + D_FN

HY_ORDER = 2
HY_SHORT_CONV = 3
HY_BANDS = 16
HY_EMB_DIM = 1 + 2 * HY_BANDS
HY_FILTER_HIDDEN = 64
HY_DECAY_TARGET = 1e-2
HY_FAST_DECAY_PCT = 0.3
HY_SLOW_DECAY_PCT = 1.5
D_HY_PROJ = (HY_ORDER + 1) * D_HY

HG_HEAD_DIM = 128
HG_HEADS = D_HG // HG_HEAD_DIM
HG_CHUNK = 64
HG_PROJ = 5 * D_HG

FN_GROUPS = 4
FN_GROUP_DIM = D_FN // FN_GROUPS

D_PROJ = D_HY_PROJ + HG_PROJ + D_FN

N_EXPERTS_2 = 16
N_GROUPS = 4
EXPERTS_PER_GROUP = N_EXPERTS_2 // N_GROUPS
D_EXPERT = 512

N_MOD = 6
RMS_EPS = 1e-6
POS_BASE = 10000.0


def rmsnorm_2(x, g):
    xf = x.astype(jnp.float32)
    y = xf * lax.rsqrt(jnp.mean(xf * xf, axis=-1, keepdims=True) + RMS_EPS)
    return (y * g.astype(jnp.float32)).astype(x.dtype)

def modulate(h, shift, scale):
    return h * (1 + scale) + shift

def ada_modulation_2(cond, w, b):
    return jnp.split(jax.nn.silu(cond) @ w + b, N_MOD, axis=-1)

def grid_sincos(n_tok):
    rows = n_tok // GRID_W
    row = jnp.repeat(jnp.arange(rows, dtype=jnp.float32), GRID_W)
    col = jnp.tile(jnp.arange(GRID_W, dtype=jnp.float32), rows)
    quarter = D_MODEL // 4
    omega = 1.0 / (POS_BASE ** (jnp.arange(quarter, dtype=jnp.float32) / quarter))
    ar = row[:, None] * omega
    ac = col[:, None] * omega
    return jnp.concatenate([jnp.sin(ar), jnp.cos(ar), jnp.sin(ac), jnp.cos(ac)], axis=-1)

def short_conv3(u, w, b):
    up = jnp.pad(u, ((0, 0), (1, 1), (0, 0)))
    return up[:, :-2] * w[0] + up[:, 1:-1] * w[1] + up[:, 2:] * w[2] + b

def hyena_deltas():
    max_decay = math.log(HY_DECAY_TARGET) / HY_FAST_DECAY_PCT
    min_decay = math.log(HY_DECAY_TARGET) / HY_SLOW_DECAY_PCT
    return jnp.linspace(min_decay, max_decay, D_HY, dtype=jnp.float32)

def hyena_filters(L, w1, b1, w2, b2, w3, freq):
    f32 = jnp.float32
    t = jnp.linspace(0.0, 1.0, L, dtype=f32)[:, None]
    w = 2.0 * math.pi * jnp.arange(L, dtype=f32)[:, None] / L
    bands = jnp.linspace(1e-4, HY_BANDS - 1, HY_BANDS, dtype=f32)[None, :]
    z = jnp.concatenate([t, jnp.cos(bands * w), -jnp.sin(bands * w)], axis=-1)
    fr = freq.astype(f32)
    h = jnp.sin(fr * (z @ w1.astype(f32) + b1.astype(f32)))
    h = jnp.sin(fr * (h @ w2.astype(f32) + b2.astype(f32)))
    h = (h @ w3.astype(f32)).reshape(L, 2 * HY_ORDER, D_HY)
    decay = jnp.exp(-t[:, :, None] * jnp.abs(hyena_deltas()))
    return h * decay

def bidir_fftconv(u, h_fwd, h_bwd, skip):
    L, C = h_fwd.shape
    k = jnp.concatenate([h_fwd, jnp.zeros((1, C), jnp.float32), h_bwd[1:][::-1]], axis=0)
    uf = jnp.fft.rfft(u.astype(jnp.float32), n=2 * L, axis=1)
    kf = jnp.fft.rfft(k, n=2 * L, axis=0)
    y = jnp.fft.irfft(uf * kf[None], n=2 * L, axis=1)[:, :L]
    return (y + u.astype(jnp.float32) * skip.astype(jnp.float32)).astype(u.dtype)

def hyena_mixer(z, conv_w, conv_b, w1, b1, w2, b2, w3, freq, bias, norm_g):
    L = z.shape[1]
    u = short_conv3(z, conv_w, conv_b)
    v, x1, x2 = jnp.split(u, HY_ORDER + 1, axis=-1)
    h = hyena_filters(L, w1, b1, w2, b2, w3, freq)
    y = x1 * bidir_fftconv(v, h[:, 0], h[:, 1], bias[0])
    y = x2 * bidir_fftconv(y, h[:, 2], h[:, 3], bias[1])
    return rmsnorm_2(y, norm_g)

def fourier_mixer(z, w, b, norm_g):
    B, L, _ = z.shape
    zg = z.astype(jnp.float32).reshape(B, L, FN_GROUPS, FN_GROUP_DIM)
    y = jnp.fft.fftn(zg, axes=(1, 3), norm="ortho").real
    y = jnp.einsum("blgc,gcd->blgd", y, w.astype(jnp.float32)).reshape(B, L, D_FN) + b.astype(jnp.float32)
    return rmsnorm_2(y.astype(z.dtype), norm_g)

def hgrn_lower_bounds(raw):
    cs = jnp.cumsum(jax.nn.softmax(raw.astype(jnp.float32), axis=0), axis=0)
    return cs - cs[0:1]

def hgrn2_inputs(z, lb):
    B, L, _ = z.shape
    q, f_fwd, f_bwd, i, g = jnp.split(z.astype(jnp.float32), 5, axis=-1)
    heads = lambda t: t.reshape(B, L, HG_HEADS, HG_HEAD_DIM)
    q = heads(jax.nn.silu(q)) * (HG_HEAD_DIM ** -0.5)
    dirs = []
    for d, f_raw in enumerate((f_fwd, f_bwd)):
        lbd = lb[d]
        forget = lbd + (1.0 - lbd) * jax.nn.sigmoid(f_raw)
        dirs.append((heads(1.0 - forget), heads(jnp.log(forget))))
    return q, heads(i), g, dirs

def to_chunks(t):
    B, L, H, d = t.shape
    return t.reshape(B, L // HG_CHUNK, HG_CHUNK, H, d).transpose(1, 0, 3, 2, 4)

def from_chunks(t):
    n, B, H, C, d = t.shape
    return t.transpose(1, 0, 3, 2, 4).reshape(B, n * C, H, d)

def gla_chunk_scan(q, k, v, logf, s0):
    causal = jnp.tril(jnp.ones((HG_CHUNK, HG_CHUNK), dtype=bool))

    def step(s, inp):
        qc, kc, vc, gc = inp
        b = jnp.cumsum(gc, axis=2)
        o_inter = jnp.einsum("bhtd,bhdv->bhtv", qc * jnp.exp(b), s)
        diff = b[:, :, :, None, :] - b[:, :, None, :, :]
        decay = jnp.exp(jnp.where(causal[:, :, None], diff, -jnp.inf))
        scores = jnp.einsum("bhtd,bhsd,bhtsd->bhts", qc, kc, decay)
        o_intra = jnp.einsum("bhts,bhsv->bhtv", scores, vc)
        b_end = b[:, :, -1, :]
        s_new = jnp.exp(b_end)[..., None] * s + jnp.einsum(
            "bhsd,bhsv->bhdv", kc * jnp.exp(b_end[:, :, None, :] - b), vc)
        return s_new, o_inter + o_intra

    s_fin, o = lax.scan(step, s0, (to_chunks(q), to_chunks(k), to_chunks(v), to_chunks(logf)))
    return s_fin, from_chunks(o)

def hgrn2_bidir(q, v, dirs, s0_fwd, s0_bwd):
    (k_f, g_f), (k_b, g_b) = dirs
    s_f, o_f = gla_chunk_scan(q, k_f, v, g_f, s0_fwd)
    flip = lambda t: t[:, ::-1]
    s_b, o_b = gla_chunk_scan(flip(q), flip(k_b), flip(v), flip(g_b), s0_bwd)
    return s_f, s_b, o_f + flip(o_b)

def hgrn2_readout(o, g, norm_g):
    B, L, H, d = o.shape
    on = o * lax.rsqrt(jnp.mean(o * o, axis=-1, keepdims=True) + RMS_EPS)
    return on.reshape(B, L, D_HG) * norm_g.astype(jnp.float32) * jax.nn.silu(g)

def mixer_output(z, o_hg, g_hg, w_out, conv_w, conv_b, w1, b1, w2, b2, w3, freq,
                 hy_bias, hy_norm_g, hg_norm_g, fn_w, fn_b, fn_norm_g):
    y_hy = hyena_mixer(z[..., :D_HY_PROJ], conv_w, conv_b, w1, b1, w2, b2, w3, freq, hy_bias, hy_norm_g)
    y_hg = hgrn2_readout(o_hg, g_hg, hg_norm_g).astype(z.dtype)
    y_fn = fourier_mixer(z[..., D_HY_PROJ + HG_PROJ:], fn_w, fn_b, fn_norm_g)
    return jnp.concatenate([y_hy, y_hg, y_fn], axis=-1) @ w_out

def moe_ffn(h, router_w, router_b, w_gate, w_up, w_down):
    N = h.shape[0]
    probs = jax.nn.softmax(h.astype(jnp.float32) @ router_w.astype(jnp.float32), axis=-1)
    sel = probs + router_b.astype(jnp.float32)
    group_score = lax.top_k(sel.reshape(N, N_GROUPS, EXPERTS_PER_GROUP), TOP_K)[0].sum(-1)
    best_group = jnp.argmax(group_score, axis=-1)
    in_group = (jnp.arange(N_EXPERTS_2) // EXPERTS_PER_GROUP)[None, :] == best_group[:, None]
    _, idx = lax.top_k(jnp.where(in_group, sel, -jnp.inf), TOP_K)
    gp = jnp.take_along_axis(probs, idx, axis=-1)
    gp = gp / jnp.sum(gp, axis=-1, keepdims=True)
    combine = jnp.sum(jax.nn.one_hot(idx, N_EXPERTS_2, dtype=jnp.float32) * gp[..., None], axis=1)
    out = jnp.zeros(h.shape, jnp.float32)
    for e in range(N_EXPERTS_2):
        he = (jax.nn.silu(h @ w_gate[e]) * (h @ w_up[e])) @ w_down[e]
        out = out + combine[:, e:e + 1] * he.astype(jnp.float32)
    return out.astype(h.dtype)

def second_inputs(seed: int = 0) -> dict:
    key = jax.random.key(seed)
    ks = jax.random.split(key, 32)
    f32 = jnp.float32
    nrm = lambda k, shape, s: s * jax.random.normal(k, shape, f32)
    D = D_MODEL
    return {
        "x": nrm(ks[0], (BATCH, SEQ, D), 1.0),
        "c": nrm(ks[1], (BATCH, D), 1.0),
        "ctx": nrm(ks[2], (BATCH, CTX_LEN, D), 1.0),
        "c_ctx": nrm(ks[3], (D,), 1.0),
        "ada_w": nrm(ks[4], (DEPTH_2, D, N_MOD * D), 0.5 * D ** -0.5),
        "ada_b": nrm(ks[5], (DEPTH_2, N_MOD * D), 0.02),
        "norm1_g": 1.0 + nrm(ks[6], (DEPTH_2, D), 0.1),
        "norm2_g": 1.0 + nrm(ks[7], (DEPTH_2, D), 0.1),
        "w_in": nrm(ks[8], (DEPTH_2, D, D_PROJ), D ** -0.5),
        "w_out": nrm(ks[9], (DEPTH_2, D_MIX, D), D_MIX ** -0.5),
        "hy_conv_w": nrm(ks[10], (DEPTH_2, HY_SHORT_CONV, D_HY_PROJ), 0.5),
        "hy_conv_b": nrm(ks[11], (DEPTH_2, D_HY_PROJ), 0.02),
        "hy_filt_w1": nrm(ks[12], (DEPTH_2, HY_EMB_DIM, HY_FILTER_HIDDEN), HY_EMB_DIM ** -0.5),
        "hy_filt_b1": nrm(ks[13], (DEPTH_2, HY_FILTER_HIDDEN), 0.02),
        "hy_filt_w2": nrm(ks[14], (DEPTH_2, HY_FILTER_HIDDEN, HY_FILTER_HIDDEN), HY_FILTER_HIDDEN ** -0.5),
        "hy_filt_b2": nrm(ks[15], (DEPTH_2, HY_FILTER_HIDDEN), 0.02),
        "hy_filt_w3": nrm(ks[16], (DEPTH_2, HY_FILTER_HIDDEN, 2 * HY_ORDER * D_HY), HY_FILTER_HIDDEN ** -0.5),
        "hy_filt_freq": 1.0 + nrm(ks[17], (DEPTH_2, HY_FILTER_HIDDEN), 0.1),
        "hy_bias": nrm(ks[18], (DEPTH_2, HY_ORDER, D_HY), 0.5),
        "hy_norm_g": 1.0 + nrm(ks[19], (DEPTH_2, D_HY), 0.1),
        "hg_lower_bounds": nrm(ks[20], (DEPTH_2, 2, D_HG), 1.0),
        "hg_norm_g": 1.0 + nrm(ks[21], (DEPTH_2, D_HG), 0.1),
        "fn_w": nrm(ks[22], (DEPTH_2, FN_GROUPS, FN_GROUP_DIM, FN_GROUP_DIM), FN_GROUP_DIM ** -0.5),
        "fn_b": nrm(ks[23], (DEPTH_2, D_FN), 0.02),
        "fn_norm_g": 1.0 + nrm(ks[24], (DEPTH_2, D_FN), 0.1),
        "router_w": nrm(ks[25], (D, N_EXPERTS_2), D ** -0.5),
        "router_b": nrm(ks[26], (N_EXPERTS_2,), 0.01),
        "moe_w_gate": nrm(ks[27], (DEPTH_2, N_EXPERTS_2, D, D_EXPERT), D ** -0.5),
        "moe_w_up": nrm(ks[28], (DEPTH_2, N_EXPERTS_2, D, D_EXPERT), D ** -0.5),
        "moe_w_down": nrm(ks[29], (DEPTH_2, N_EXPERTS_2, D_EXPERT, D), D_EXPERT ** -0.5),
        "final_norm_g": 1.0 + nrm(ks[30], (D,), 0.1),
    }

def second_block(x, c, ctx, c_ctx, ada_w, ada_b, norm1_g, norm2_g, w_in, w_out, hy_conv_w, hy_conv_b,
              hy_filt_w1, hy_filt_b1, hy_filt_w2, hy_filt_b2, hy_filt_w3, hy_filt_freq, hy_bias, hy_norm_g,
              hg_lower_bounds, hg_norm_g, fn_w, fn_b, fn_norm_g, router_w, router_b,
              moe_w_gate, moe_w_up, moe_w_down, final_norm_g):
    B, L, D = x.shape
    n_ctx = ctx.shape[1]
    lower_bounds = hgrn_lower_bounds(hg_lower_bounds)
    x = x + grid_sincos(L).astype(x.dtype)[None]
    cond_x = c[:, None, :]
    cond_c = c_ctx[None, None, :]
    s_zero = jnp.zeros((B, HG_HEADS, HG_HEAD_DIM, HG_HEAD_DIM), jnp.float32)
    hg_lo, hg_hi = D_HY_PROJ, D_HY_PROJ + HG_PROJ
    for layer in range(DEPTH_2):
        last = layer == DEPTH_2 - 1
        mod_x = ada_modulation_2(cond_x, ada_w[layer], ada_b[layer])
        mod_c = ada_modulation_2(cond_c, ada_w[layer], ada_b[layer])
        mix_params = (w_out[layer], hy_conv_w[layer], hy_conv_b[layer], hy_filt_w1[layer], hy_filt_b1[layer],
                      hy_filt_w2[layer], hy_filt_b2[layer], hy_filt_w3[layer], hy_filt_freq[layer],
                      hy_bias[layer], hy_norm_g[layer], hg_norm_g[layer], fn_w[layer], fn_b[layer], fn_norm_g[layer])
        hx = modulate(rmsnorm_2(x, norm1_g[layer]), mod_x[0], mod_x[1])
        hc = modulate(rmsnorm_2(ctx, norm1_g[layer]), mod_c[0], mod_c[1])
        zx = hx @ w_in[layer]
        zc = hc @ w_in[layer]
        q_c, v_c, g_c, dirs_c = hgrn2_inputs(zc[..., hg_lo:hg_hi], lower_bounds[layer])
        s_f, s_b, o_c = hgrn2_bidir(q_c, v_c, dirs_c, s_zero, s_zero)
        q_x, v_x, g_x, dirs_x = hgrn2_inputs(zx[..., hg_lo:hg_hi], lower_bounds[layer])
        _, _, o_x = hgrn2_bidir(q_x, v_x, dirs_x, s_f, s_b)
        x = x + mod_x[2] * mixer_output(zx, o_x, g_x, *mix_params)
        hx2 = modulate(rmsnorm_2(x, norm2_g[layer]), mod_x[3], mod_x[4])
        if last:
            ff_x = moe_ffn(hx2.reshape(B * L, D), router_w, router_b,
                           moe_w_gate[layer], moe_w_up[layer], moe_w_down[layer])
        else:
            ctx = ctx + mod_c[2] * mixer_output(zc, o_c, g_c, *mix_params)
            hc2 = modulate(rmsnorm_2(ctx, norm2_g[layer]), mod_c[3], mod_c[4])
            ff = moe_ffn(jnp.concatenate([hc2.reshape(B * n_ctx, D), hx2.reshape(B * L, D)], axis=0),
                         router_w, router_b, moe_w_gate[layer], moe_w_up[layer], moe_w_down[layer])
            ctx = ctx + mod_c[5] * ff[:B * n_ctx].reshape(B, n_ctx, D)
            ff_x = ff[B * n_ctx:]
        x = x + mod_x[5] * ff_x.reshape(B, L, D)
    return rmsnorm_2(x, final_norm_g)


def setup_inputs(seed=0):
    out = dict(first_inputs(seed))
    for name, value in second_inputs(seed + 1).items():
        if name != "x":
            out[name + "_2"] = value
    return out


def reference(
    x, c, positions, ada_w, ada_b, norm_mix, norm_ffn, norm_final, w_in, tshift_mu, w0, w_up,
    a0, a_up, g_up, k_k, k_a, r_k, lnx_g, lnx_b, rwkv_out, q_norm, w_qb, kv_norm, w_kvb,
    mla_out, w_o, ffn_w1, ffn_w3, ffn_w2, router_w, router_b, moe_w1, moe_w3, moe_w2, c_2,
    ctx_2, c_ctx_2, ada_w_2, ada_b_2, norm1_g_2, norm2_g_2, w_in_2, w_out_2, hy_conv_w_2,
    hy_conv_b_2, hy_filt_w1_2, hy_filt_b1_2, hy_filt_w2_2, hy_filt_b2_2, hy_filt_w3_2,
    hy_filt_freq_2, hy_bias_2, hy_norm_g_2, hg_lower_bounds_2, hg_norm_g_2, fn_w_2, fn_b_2,
    fn_norm_g_2, router_w_2, router_b_2, moe_w_gate_2, moe_w_up_2, moe_w_down_2, final_norm_g_2,
):
    x = first_block(
        x, c, positions, ada_w, ada_b, norm_mix, norm_ffn, norm_final, w_in, tshift_mu, w0,
        w_up, a0, a_up, g_up, k_k, k_a, r_k, lnx_g, lnx_b, rwkv_out, q_norm, w_qb, kv_norm,
        w_kvb, mla_out, w_o, ffn_w1, ffn_w3, ffn_w2, router_w, router_b, moe_w1, moe_w3, moe_w2,
    )
    return second_block(
        x, c_2, ctx_2, c_ctx_2, ada_w_2, ada_b_2, norm1_g_2, norm2_g_2, w_in_2, w_out_2,
        hy_conv_w_2, hy_conv_b_2, hy_filt_w1_2, hy_filt_b1_2, hy_filt_w2_2, hy_filt_b2_2,
        hy_filt_w3_2, hy_filt_freq_2, hy_bias_2, hy_norm_g_2, hg_lower_bounds_2, hg_norm_g_2,
        fn_w_2, fn_b_2, fn_norm_g_2, router_w_2, router_b_2, moe_w_gate_2, moe_w_up_2,
        moe_w_down_2, final_norm_g_2,
    )


_drawn_inputs = setup_inputs


def setup_inputs(seed=0):
    import zlib

    import numpy as np

    out = dict(_drawn_inputs(seed))
    spreads = {}
    factors = {'norm_mix': 2.915,
     'w_up': 3.252,
     'a0': 4.978,
     'k_k': 6.06,
     'k_a': 3.219,
     'lnx_g': 5.478,
     'lnx_b': 8.0,
     'q_norm': 8.0,
     'kv_norm': 8.0,
     'router_b': 24.193,
     'ctx_2': 27.308,
     'c_ctx_2': 8.0,
     'hy_conv_b_2': 8.0,
     'hy_filt_b2_2': 3.877,
     'hy_bias_2': 3.299,
     'hy_norm_g_2': 5.749,
     'hg_norm_g_2': 3.686,
     'fn_b_2': 4.459,
     'fn_norm_g_2': 3.701}
    for name, (base, spread) in spreads.items():
        noise = np.random.default_rng([zlib.crc32(name.encode()), seed]).standard_normal(out[name].shape)
        drawn = base * np.exp(spread * noise) if base else spread * noise
        out[name] = __import__('jax').numpy.asarray(drawn.astype(out[name].dtype))
    for name, factor in factors.items():
        out[name] = (out[name] * factor).astype(out[name].dtype)
    return out
```

```python
import math

import numpy as np

import concourse.bass as bass
from concourse import mybir
from concourse.alu_op_type import AluOpType as ALU

F32 = mybir.dt.float32
I32 = mybir.dt.int32
ACT = mybir.ActivationFunctionType
AX = mybir.AxisListType

S = 256
D = 1024
KD = D // 128
CHUNK = 64
DEPTH = 2
RW, RT = 512, 4
HEADS = 8
SHIFT_T = 14
IN_T = 36
QL_T, KV_T = 3, 2
NOPE, ROPE = 64, 32
QK = NOPE + ROPE
D_FF, E1, F1 = 2816, 8, 3584
E2, F2 = 16, 512
GROUP = 256
IN2_T = 28
CHUNK_COLS = 2048
WIDE = 128
RING = 6
DECAY_SCALE = math.exp(-0.5)
EPS = 1e-6
ARENA = 26400
TWO_PI = 2.0 * math.pi


VEC_TILES = [("c", 8), ("c_2", 8), ("c_ctx_2", 8)]
for _l in range(DEPTH):
    VEC_TILES += [(f"ada_b{_l}0", 24), (f"ada_b{_l}1", 24), (f"norm_mix{_l}", 8), (f"norm_ffn{_l}", 8),
                  (f"mu{_l}", 14), (f"w0{_l}", 4), (f"a0{_l}", 4), (f"k_k{_l}", 4), (f"k_a{_l}", 4),
                  (f"r_k{_l}", 4), (f"lnx_g{_l}", 4), (f"lnx_b{_l}", 4), (f"q_norm{_l}", 3),
                  (f"kv_norm{_l}", 2)]
VEC_TILES += [("norm_final", 8), ("ada_b_2", 48), ("norm1_g_2", 8), ("norm2_g_2", 8), ("conv_w0", 6),
              ("conv_w1", 6), ("conv_w2", 6), ("conv_b", 6), ("filt_b1", 1), ("filt_b2", 1),
              ("filt_freq", 1), ("hy_bias0", 2), ("hy_bias1", 2), ("hy_norm_g_2", 2), ("lb_f", 4),
              ("lb_b", 4), ("hg_norm_g_2", 4), ("fn_b_2", 2), ("fn_norm_g_2", 2), ("final_norm_g_2", 8),
              ("router_b", E1), ("router_b_2", E2), ("router_w", KD * E1), ("router_w_2", KD * E2),
              ("inv_freq", 1), ("filt_w1", 64), ("filt_w2", 64), ("filt_w3", 1024), ("fn_w", 128)]
VEC_AT, _n = {}, 0
for _name, _t in VEC_TILES:
    VEC_AT[_name] = (_n, _t)
    _n += _t
VEC_COLS = _n

LEVELS = [1, 2, 4, 8, 16, 32, 64]
CONST_TILES = [("ident", 128), ("ones", 128), ("headsum", 128), ("swap", 32),
               ("low", 128), ("upp", 128), ("uppeq", 128)]
CONST_TILES += [(f"lv{m}", 128) for m in LEVELS] + [(f"lvT{m}", 128) for m in LEVELS]
CONST_TILES += [("start", S), ("causal", 384), ("sign", 1), ("halfident", 64), ("iota", 16), ("group", 16),
                ("tri", 128), ("slots", 128), ("eps", 3)]
CONST_AT, _n = {}, 0
for _name, _t in CONST_TILES:
    CONST_AT[_name] = (_n, _t)
    _n += _t
CONST_COLS = _n
LATE_TILES = [("pos", KD * S), ("oddC", 2 * S), ("oddS", 2 * S), ("oddCT", 2 * S), ("oddST", 2 * S),
              ("fC", 2 * S), ("fS", 2 * S), ("gC", 128), ("gS", 128), ("z", S), ("hdecay", 2 * S),
              ("run64", S), ("run128", S), ("run256", S)]
LATE_AT, _n = {}, 0
for _name, _t in LATE_TILES:
    LATE_AT[_name] = (_n, _t)
    _n += _t
LATE_COLS = _n


def constants():
    p, q = np.arange(128)[:, None], np.arange(128)[None, :]
    same = (p // CHUNK) == (q // CHUNK)
    out = {
        "ident": p == q, "ones": np.ones((128, 128)), "headsum": same,
        "low": same & (q < p), "upp": same & (p < q), "uppeq": same & (p <= q),
    }
    swap = np.zeros((128, 32))
    for i in range(32):
        swap[64 + (i + 16) % 32, i] = 1
    out["swap"] = swap
    for m in LEVELS:
        lv = (p // (2 * m) == q // (2 * m)) & (p // m % 2 == 1) & (q // m % 2 == 0)
        out[f"lv{m}"] = lv
        out[f"lvT{m}"] = lv.T
    t = np.arange(S)[None, :]
    out["start"] = np.broadcast_to(t % CHUNK == 0, (128, S))
    seen = [t // CHUNK <= (128 * b + p) // CHUNK for b in range(2)]
    out["causal"] = np.where(np.concatenate([seen[0][:, :128], seen[1]], 1), 0.0, -1e30)
    out["sign"] = np.where((p // 16) % 2 == 0, -1.0, 1.0)
    out["iota"] = np.broadcast_to(np.arange(16), (128, 16))
    out["group"] = np.broadcast_to(np.arange(16) // 4, (128, 16))
    out["tri"] = p <= q
    out["slots"] = np.broadcast_to(np.arange(128), (128, 128))
    out["eps"] = np.broadcast_to(np.array([EPS, 1e-12, 64e-5]), (128, 3))
    out["halfident"] = p % 64 == np.arange(64)[None]
    return np.concatenate([np.asarray(out[n], np.float32).reshape(128, w) for n, w in CONST_TILES], 1)


def tiles_of(a):
    n = a.shape[0] // 128
    return a.reshape(n, 128, -1).transpose(1, 0, 2).reshape(128, -1)


def late_constants():
    f = np.float32
    quarter = D // 4
    rows, cols = np.repeat(np.arange(S // 64), 64), np.tile(np.arange(64), S // 64)
    omega = (1.0 / 10000.0 ** (np.arange(quarter) / quarter))
    ar, ac = rows[:, None] * omega, cols[:, None] * omega
    pos = np.concatenate([np.sin(ar), np.cos(ar), np.sin(ac), np.cos(ac)], -1)
    t = np.arange(S)
    theta = np.pi * np.outer(2 * t + 1, t) / 512.0
    full = 2 * np.pi * np.outer(t, t) / S
    g = 2 * np.pi * np.outer(np.arange(64), np.arange(64)) / 64
    gC, gS = np.zeros((128, 128)), np.zeros((128, 128))
    for i in range(2):
        gC[64 * i:64 * i + 64, 64 * i:64 * i + 64] = np.cos(g) / 128.0
        gS[64 * i:64 * i + 64, 64 * i:64 * i + 64] = np.sin(g) / 128.0
    tl = np.linspace(0.0, 1.0, S)
    w = 2.0 * math.pi * t / S
    bands = np.linspace(1e-4, 15, 16)
    z = np.zeros((128, S))
    z[0] = tl
    z[1:17] = np.cos(bands[:, None] * w)
    z[17:33] = -np.sin(bands[:, None] * w)
    deltas = np.linspace(math.log(1e-2) / 1.5, math.log(1e-2) / 0.3, 256)
    hdecay = np.exp(-tl[:, None] * np.abs(deltas)[None])
    out = {
        "pos": tiles_of(pos.T), "oddC": tiles_of(np.cos(theta)), "oddS": tiles_of(np.sin(theta)),
        "oddCT": tiles_of(np.cos(theta).T), "oddST": tiles_of(np.sin(theta).T),
        "fC": tiles_of(np.cos(full)), "fS": tiles_of(np.sin(full)), "gC": gC, "gS": gS, "z": z,
        "hdecay": tiles_of(hdecay),
        "run64": np.broadcast_to(t % 64 != 0, (128, S)),
        "run128": np.broadcast_to(t % 128 != 0, (128, S)),
        "run256": np.broadcast_to(t != 0, (128, S)),
    }
    return np.concatenate([np.asarray(out[n], f).reshape(128, w) for n, w in LATE_TILES], 1)


def vectors(i):
    f = np.float32
    def pad(a, rows=128):
        return np.concatenate([a, np.zeros((rows - a.shape[0],) + a.shape[1:], f)], 0)
    v = {"c": i["c"][0], "c_2": i["c_2"][0], "c_ctx_2": i["c_ctx_2"]}
    for l in range(DEPTH):
        v[f"ada_b{l}0"], v[f"ada_b{l}1"] = i["ada_b"][l, 0], i["ada_b"][l, 1]
        for name, key in (("norm_mix", "norm_mix"), ("norm_ffn", "norm_ffn"), ("mu", "tshift_mu"),
                          ("w0", "w0"), ("a0", "a0"), ("k_k", "k_k"), ("k_a", "k_a"), ("r_k", "r_k"),
                          ("lnx_g", "lnx_g"), ("lnx_b", "lnx_b"), ("q_norm", "q_norm"),
                          ("kv_norm", "kv_norm")):
            v[f"{name}{l}"] = i[key][l].reshape(-1)
    v["norm_final"] = i["norm_final"]
    v["ada_b_2"] = i["ada_b_2"][0]
    for name in ("norm1_g_2", "norm2_g_2", "hy_norm_g_2", "hg_norm_g_2", "fn_b_2", "fn_norm_g_2"):
        v[name] = i[name][0]
    for n in range(3):
        v[f"conv_w{n}"] = i["hy_conv_w_2"][0, n]
    v["conv_b"] = i["hy_conv_b_2"][0]
    v["filt_b1"], v["filt_b2"] = pad(i["hy_filt_b1_2"][0]), pad(i["hy_filt_b2_2"][0])
    v["filt_freq"] = pad(i["hy_filt_freq_2"][0])
    v["hy_bias0"], v["hy_bias1"] = i["hy_bias_2"][0, 0], i["hy_bias_2"][0, 1]
    v["lb_f"], v["lb_b"] = i["hg_lower_bounds_2"][0, 0], i["hg_lower_bounds_2"][0, 1]
    v["final_norm_g_2"] = i["final_norm_g_2"]
    inv = (10000.0 ** (-np.arange(0, ROPE, 2, dtype=f) / f(ROPE))).astype(f)
    v["inv_freq"] = np.tile(inv, 8)
    v = {n: tiles_of(a.reshape(-1, 1)) for n, a in v.items()}
    v["router_b"] = np.broadcast_to(i["router_b"][0][None], (128, E1))
    v["router_b_2"] = np.broadcast_to(i["router_b_2"][None], (128, E2))
    v["router_w"] = tiles_of(i["router_w"][0])
    v["router_w_2"] = tiles_of(i["router_w_2"])
    v["filt_w1"], v["filt_w2"] = pad(i["hy_filt_w1_2"][0]), pad(i["hy_filt_w2_2"][0])
    v["filt_w3"] = pad(i["hy_filt_w3_2"][0])
    fn = i["fn_w_2"][0]
    v["fn_w"] = np.concatenate([fn[0::2].reshape(2, 64, 64).transpose(1, 0, 2).reshape(64, 128),
                                fn[1::2].reshape(2, 64, 64).transpose(1, 0, 2).reshape(64, 128)], 0)
    return np.concatenate([v[n].reshape(128, w) for n, w in VEC_TILES], 1).astype(f)


def columns(w, cols=None):
    k, n = w.shape
    per = CHUNK_COLS // (k // 128)
    return w.reshape(k // 128, 128, n // per, per).transpose(2, 1, 0, 3).reshape(n // per, 128, CHUNK_COLS)


def rows(w):
    return w.reshape(-1, 2, 128, D).transpose(0, 2, 1, 3).reshape(-1, 128, CHUNK_COLS)


def padded(a):
    return np.concatenate([a, np.zeros((128, CHUNK_COLS - a.shape[1]), np.float32)], 1)[None]


def ffn_stream(w1, w3, w2):
    a, b, c = columns(w1), columns(w3), rows(w2)
    out = []
    for g in range(0, len(a), 2):
        two = range(g, min(g + 2, len(a)))
        for n in two:
            out += [a[n:n + 1], b[n:n + 1]]
        for n in two:
            out.append(c[n:n + 1])
    return out


ADA_CH, IN_CH, QB_CH, OUT_CH, WO_CH = 12, IN_T // 2, 2, 2, 4
ADA2_CH = 24
MLA_FILL = 3
SS_CH = 8
MIX_CH = IN_CH + 1 + OUT_CH + QB_CH + 1 + OUT_CH + WO_CH
FFN_CH = 3 * D_FF // GROUP
ALIGN_0 = 2 * MIX_CH + 4 * ADA_CH + SS_CH + FFN_CH
PAD_1 = -ALIGN_0 % RING
MOE1_CH = E1 * 3 * F1 // GROUP
BLOCK2_CH = IN2_T // 2 + ADA2_CH - SS_CH + WO_CH
PAD_2 = -BLOCK2_CH % RING
MOE2_CH = E2 * 3 * F2 // GROUP
STREAM_CH = ALIGN_0 + PAD_1 + MOE1_CH + BLOCK2_CH + PAD_2 + MOE2_CH
assert STREAM_CH % RING == 0


def stream(i):
    parts = []
    blank = np.zeros((1, 128, CHUNK_COLS), np.float32)
    parts.append(columns(i["ada_w"][0, 0])[:SS_CH])
    for l in range(DEPTH):
        w = i["w_in"][l]
        zero = np.zeros((D, 64), np.float32)
        sh = 1792
        kv_end = sh + 384 + 256
        w = np.concatenate([w[:, :kv_end], zero, w[:, kv_end:kv_end + ROPE], zero[:, :32],
                            w[:, kv_end + ROPE:]], 1)
        parts.append(columns(w))
        lora = np.concatenate([i["g_up"][l], np.concatenate([i["w_up"][l], i["a_up"][l]], 0)], 1)
        parts.append(padded(lora))
        parts.append(columns(i["ada_w"][l, 0])[SS_CH:])
        parts.append(columns(i["ada_w"][l, 1]))
        parts.append(columns(i["ada_w"][1, 0] if l == 0 else i["ada_w_2"][0])[:SS_CH])
        last = parts.pop()
        parts += [last[:-MLA_FILL], columns(i["rwkv_out"][l]), last[-MLA_FILL:]]
        qb = i["w_qb"][l].reshape(3, 128, 2, 4 * QK).transpose(2, 1, 0, 3).reshape(2, 128, -1)
        parts += [padded(qb[0]), padded(qb[1])]
        parts.append(padded(tiles_of(i["w_kvb"][l])))
        parts.append(columns(i["mla_out"][l]))
        parts.append(columns(i["w_o"][l]))
        if l == 0:
            parts += ffn_stream(i["ffn_w1"][0], i["ffn_w3"][0], i["ffn_w2"][0])
    parts += [blank] * PAD_1
    for e in range(E1):
        parts += ffn_stream(i["moe_w1"][0, e], i["moe_w3"][0, e], i["moe_w2"][0, e])
    parts.append(columns(i["w_in_2"][0]))
    parts.append(columns(i["ada_w_2"][0])[SS_CH:])
    parts.append(columns(i["w_out_2"][0]))
    parts += [blank] * PAD_2
    for e in range(0, E2, 2):
        a, b = [ffn_stream(i["moe_w_gate_2"][0, n], i["moe_w_up_2"][0, n], i["moe_w_down_2"][0, n])
                for n in (e, e + 1)]
        parts += a[:4] + b[:2] + a[4:] + b[2:]
    out = np.concatenate(parts, 0)
    assert out.shape[0] == STREAM_CH, (out.shape, STREAM_CH)
    return out


class Signal:

    def __init__(self, handle):
        self.handle, self.count = handle, 0

    def next(self, by=1):
        self.count += by
        return self.handle, by

    def all(self):
        return self.handle, self.count


def build(nc, vec_in, const_in, late_in, stream_in, x_in, ctx_in, pos_in, fin_out, debug=None):
    from contextlib import ExitStack

    ctx = ExitStack()
    with ctx:
        def sb(name, shape, dt=F32):
            return ctx.enter_context(nc.sbuf_tensor(name, shape, dt))

        def signal(name):
            return Signal(ctx.enter_context(nc.semaphore(name)))

        ring = sb("ring", [128, RING, CHUNK_COLS])
        vec = sb("vec", [128, VEC_COLS])
        const = sb("const", [128, CONST_COLS])
        late = sb("late", [128, 2048])
        xT = sb("xT", [128, KD, S])
        hT = sb("hT", [128, KD, 2 * S])
        mods = sb("mods", [128, 4, 24])
        mod2 = sb("mod2", [128, 48, 2])
        cs = sb("cs", [128, 8, 4])
        rope = sb("rope", [128, 2, S])
        comb = sb("comb", [128, 2, E2])
        weight = sb("weight", [128, 2])
        i8u = sb("i8", [128, 8], mybir.dt.uint32)
        flag = sb("flag", [1, 2], I32)
        tiny = sb("tiny", [128, 64])
        A = sb("arena", [128, ARENA])
        bank = [ctx.enter_context(nc.psum_tensor(f"bank{n}", [128, 512], F32)) for n in range(8)]

        chunk_in = [signal(f"chunk_in{n}") for n in range(RING)]
        used = signal("chunks_used")
        vec_at = signal("vec_in")
        cond_at = signal("conditions")
        small_in = signal("small_in")
        late_at = signal("late_in")
        out_at = signal("out_written")
        pe_done = signal("pe_done")
        act_done = signal("act_done")
        dve_done = signal("dve_done")
        pool_done = signal("pool_done")
        part_whole = signal("part_whole")
        evac = signal("banks_evacuated")
        silu_at = signal("silu_at")
        gated = signal("gated")
        accd = signal("accumulated")
        block = ctx.enter_context(nc.Block())

        def V(name):
            a, w = VEC_AT[name]
            return vec[:, a:a + w]

        def C(name):
            a, w = CONST_AT[name]
            return const[:, a:a + w]

        def col(name, t):
            a, _ = VEC_AT[name]
            return vec[:, a + t:a + t + 1]

        def carve(at, shape):
            n = int(np.prod(shape))
            assert at + n <= ARENA, (at, shape)
            v = A[:, at:at + n]
            if len(shape) == 2:
                v = v.rearrange("p (a b) -> p a b", a=shape[0])
            if len(shape) == 3:
                v = v.rearrange("p (a b c) -> p a b c", a=shape[0], b=shape[1])
            return v

        def over(ap, n):
            return ap.unsqueeze(1).to_broadcast([128, n, ap.shape[1]])

        def flat(ap):
            return ap.rearrange("p a b -> p (a b)")

        def two(banks):
            return [b[:, :].rearrange("p (f t) -> p f t", f=2) for b in banks]

        def link(ins):
            ins.then_inc(*dve_done.next())
            nc.vector.wait_ge(*dve_done.all())

        def alink(ins):
            ins.then_inc(*act_done.next())
            nc.scalar.wait_ge(*act_done.all())

        def mm(out, lhsT, rhs, start=True, stop=True):
            return nc.tensor.matmul(out, lhsT, rhs, start=start, stop=stop)

        ident = C("ident")
        HALVES = (slice(0, 64), slice(64, 128))
        b2, b4 = two(bank), [b[:, :].rearrange("p (a b) -> p a b", a=4) for b in bank]
        turn, tt, stt = nc.tensor.transpose, nc.vector.tensor_tensor, nc.vector.scalar_tensor_tensor
        ts, cp, act, red = (nc.vector.tensor_scalar, nc.vector.tensor_copy, nc.scalar.activation,
                            nc.vector.tensor_reduce)

        @block.sync
        def _(sp):
            for n in range(RING):
                sp.dma_start(ring[:, n, :], stream_in[n]).then_inc(chunk_in[n].handle, 16)
            with sp.Fori(1, STREAM_CH // RING) as again:
                for n in range(RING):
                    sp.wait_ge(used.handle, (again - 1) * RING + n + 1)
                    src = stream_in[bass.ds(again * RING + n, 1), :, :].rearrange("a p n -> (a p) n")
                    sp.dma_start(ring[:, n, :], src).then_inc(chunk_in[n].handle, 16)

        def take(pe):
            n = used.count
            pe.wait_ge(chunk_in[n % RING].handle, 16 * (n // RING + 1))
            return ring[:, n % RING, :]

        def skip(n):
            @block.tensor
            def _(pe):
                for _ in range(n):
                    take(pe)
                    pe.sem_inc(*used.next())

        dbg = {}
        tapped = signal("tapped") if debug is not None else None

        def tap(name, ap):
            if debug is not None and name in debug:
                shape = [128] + list(ap.shape[1:])
                t = nc.dram_tensor("dbg_" + name, (128, int(np.prod(shape[1:]))), ap.dtype,
                                   kind="ExternalOutput").ap()
                dbg[name] = shape

                @block.gpsimd
                def _(g):
                    for s in (act_done, dve_done, evac, accd, pe_done, pool_done):
                        if s.count:
                            g.wait_ge(*s.all())
                    dst = t
                    if len(ap.shape) == 3:
                        dst = t.rearrange("p (a b) -> p a b", a=ap.shape[1])
                    if len(ap.shape) == 4:
                        dst = t.rearrange("p (a b c) -> p a b c", a=ap.shape[1], b=ap.shape[2])
                    g.dma_start(dst, ap).then_inc(*tapped.next(16))
                    g.wait_ge(*tapped.all())
                for eng in (block.vector, block.scalar, block.tensor):
                    @eng
                    def _(e):
                        e.wait_ge(*tapped.all())

        def load_small():
            @block.scalar
            def _(a):
                a.dma_start(vec[:, :], vec_in).then_inc(*vec_at.next(16))
                a.wait_ge(*vec_at.all())
                for n, name in enumerate(("c", "c_2", "c_ctx_2")):
                    act(cs[:, :, n:n + 1], V(name).unsqueeze(2), ACT.Silu).then_inc(*cond_at.next())
                a.wait_ge(chunk_in[2].handle, 16)
                for dst, src in ((xT[:, :, :], x_in), (const[:, :], const_in), (hT[:, 0, 0:S], pos_in)):
                    a.dma_start(dst, src).then_inc(*small_in.next(16))

            ang, turns, posf = carve(0, [S]), carve(256, [S]), carve(512, [S])

            @block.vector
            def _(v):
                v.wait_ge(*vec_at.all())
                v.wait_ge(*small_in.all())
                link(cp(posf, hT[:, 0, 0:S].bitcast(I32)))
                link(ts(ang, posf, V("inv_freq"), None, ALU.mult))
                for n, quarter in enumerate((0.25, 0.0)):
                    wrap(rope[:, n, :], ang, turns, quarter)

            @block.scalar
            def _(a):
                a.wait_ge(*dve_done.all())
                act(rope[:, :, :], rope[:, :, :], ACT.Sin).then_inc(*act_done.next())

            @block.vector
            def _(v):
                v.wait_ge(*act_done.all())
                link(ts(rope[64:96, 1, :], rope[64:96, 1, :], C("sign")[64:96, :], None, ALU.mult))

        def wrap(out, angle, turns, quarter):
            magic = 1.5 * 2.0 ** 23
            hi = 6.28125
            mid = float((np.array([TWO_PI - hi], np.float32).view(np.uint32)
                         & np.uint32(0xFFFFF000)).view(np.float32)[0])
            lo = TWO_PI - hi - mid
            link(ts(turns, angle, 1.0 / TWO_PI, quarter, ALU.mult, ALU.add))
            link(ts(turns, turns, magic, None, ALU.add))
            link(ts(turns, turns, -magic, None, ALU.add))
            link(stt(out, turns, -hi, angle, ALU.mult, ALU.add))
            link(stt(out, turns, -mid, out, ALU.mult, ALU.add))
            link(stt(out, turns, -lo, out, ALU.mult, ALU.add))
            link(ts(out, out, TWO_PI * quarter, math.pi, ALU.add, ALU.min))
            link(ts(out, out, -math.pi, None, ALU.max))

        class Modulation:

            def __init__(self):
                self.todo = []

            def add(self, chunks, rhs, n, at):
                self.todo += [(rhs, n, at + 2 * n * c) for c in range(chunks)]

            def some(self, pe, chunks):
                for _ in range(min(chunks, len(self.todo))):
                    rhs, n, at = self.todo.pop(0)
                    w = take(pe).rearrange("p (k f) -> p k f", k=KD)
                    for f in range(2):
                        for k in range(KD):
                            last = mm(bank[7][:, at + n * f:at + n * f + WIDE],
                                      w[:, k, f * 128:f * 128 + 128], rhs[:, k, :, :],
                                      start=k == 0, stop=k == KD - 1)
                    last.then_inc(*used.next())

        def wide(c, n):
            return cs[:, :, c:c + n].unsqueeze(2).to_broadcast([128, KD, WIDE // n, n])

        modulation = Modulation()

        def fill(chunks):
            @block.tensor
            def _(pe):
                modulation.some(pe, chunks)

        def mod_of(out, at, n, bias):
            w = out.shape[1] * n

            @block.vector
            def _(v):
                v.wait_ge(*used.all())
                link(tt(out, bank[7][:, at:at + w].rearrange("p (f n) -> p f n", n=n), bias, ALU.add))

        def bias2(a, b):
            return V("ada_b_2")[:, a:b].unsqueeze(2).to_broadcast([128, b - a, 2])

        def norm(src, out, gain, shift=None, scale=None, n_tiles=KD, at=0, b=0):
            sq = carve(at, [n_tiles, S])
            rstd = carve(at + n_tiles * S, [S])
            g = tiny[:, 0:n_tiles]

            @block.scalar
            def _(a):
                a.wait_ge(*dve_done.all())
                a.wait_ge(*small_in.all())
                if evac.count:
                    a.wait_ge(*evac.all())
                if pe_done.count:
                    a.wait_ge(*pe_done.all())
                for k in range(n_tiles):
                    act(sq[:, k, :], src[:, k, :], ACT.Square).then_inc(*act_done.next())
            squares = act_done.count - n_tiles

            @block.tensor
            def _(pe):
                for k in range(n_tiles):
                    pe.wait_ge(act_done.handle, squares + k + 1)
                    last = mm(bank[b][:, 0:S], C("ones"), sq[:, k, :], start=k == 0, stop=k == n_tiles - 1)
                last.then_inc(*pe_done.next())

            @block.scalar
            def _(a):
                a.wait_ge(*pe_done.all())
                act(rstd, bank[b][:, 0:S], ACT.Sqrt, bias=C("eps")[:, 0:1],
                    scale=1.0 / (n_tiles * 128)).then_inc(*act_done.next())

            @block.vector
            def _(v):
                if scale is not None:
                    link(stt(g, scale, 1.0, gain, ALU.add, ALU.mult))
                v.wait_ge(*act_done.all())
                link(nc.vector.reciprocal(rstd, rstd))
                for k in range(n_tiles):
                    gk = (gain if scale is None else g)[:, k:k + 1]
                    stt(out[:, k, :], src[:, k, :], gk, rstd, ALU.mult, ALU.mult)\
                        .then_inc(*dve_done.next())
                v.wait_ge(*dve_done.all())
            first = dve_done.count - n_tiles
            if shift is None:
                return None

            @block.scalar
            def _(a):
                for k in range(n_tiles):
                    a.wait_ge(dve_done.handle, first + k + 1)
                    act(out[:, k, :], out[:, k, :], ACT.Identity, bias=shift[:, k:k + 1])\
                        .then_inc(*act_done.next())
            return act_done.count - n_tiles

        def project(chunks, src, k_tiles, engine, lane, reader, banks=(0, 1, 2, 3, 4, 5), tiles=None):
            c0, p0, e0 = used.count, part_whole.count, evac.count
            nb = CHUNK_COLS // (k_tiles * 128) // 2

            @block.tensor
            def _(pe):
                if tiles is None:
                    pe.wait_ge(*act_done.all())
                    pe.wait_ge(*dve_done.all())
                if e0:
                    pe.wait_ge(*evac.all())
                for c in range(chunks):
                    w = take(pe).rearrange("p (k f) -> p k f", k=k_tiles)
                    for j in range(nb):
                        n = c * nb + j
                        b = bank[banks[n % len(banks)]]
                        if n >= len(banks):
                            pe.wait_ge(evac.handle, e0 + n - len(banks) + 1)
                        for f in range(2):
                            for k in range(k_tiles):
                                if tiles is not None and n == f == 0:
                                    pe.wait_ge(act_done.handle, tiles + k + 1)
                                at = (2 * j + f) * 128
                                last = mm(b[:, f * S:f * S + S], w[:, k, at:at + 128], src[:, k, :],
                                          start=k == 0, stop=k == k_tiles - 1)
                        if j < nb - 1:
                            last.then_inc(*part_whole.next())
                    last.then_inc(*used.next())

            @engine
            def _(eng):
                for n in range(chunks * nb):
                    c, j = n // nb, n % nb
                    if j < nb - 1:
                        eng.wait_ge(part_whole.handle, p0 + c * (nb - 1) + j + 1)
                    else:
                        eng.wait_ge(used.handle, c0 + c + 1)
                    reader(bank[banks[n % len(banks)]], n).then_inc(*evac.next())

        def head_sums(src, b):
            @block.tensor
            def _(pe):
                pe.wait_ge(*dve_done.all())
                for j in range(RT):
                    last = mm(b2[b + j // 2][:, j % 2, :], C("headsum"), src[:, j, :])
                last.then_inc(*pe_done.next())

        def roots(out, b, scale, eps):
            @block.scalar
            def _(a):
                a.wait_ge(*pe_done.all())
                for j in range(2):
                    act(out[:, 2 * j:2 * j + 2, :], b2[b + j], ACT.Ln, bias=eps, scale=scale)\
                        .then_inc(*act_done.next())
                a.wait_ge(*act_done.all())
                act(out, out, ACT.Exp, scale=-0.5).then_inc(*act_done.next())

            @block.vector
            def _(v):
                v.wait_ge(*act_done.all())

        RAW = carve(0, [SHIFT_T, S + 1])
        REST = carve(3600, [22, S])
        SH = carve(9232, [SHIFT_T, S])
        GA, GB = REST[:, 6:14, :], REST[:, 14:22, :]
        R0 = 12816

        def slot(n, shape=(4, S)):
            return carve(R0 + 1024 * n, list(shape))

        def add_residual(b, n, gate):
            for f in range(2):
                ins = stt(xT[:, 2 * n + f, :], b[:, f * S:f * S + S], gate[:, 2 * n + f:2 * n + f + 1],
                          xT[:, 2 * n + f, :], ALU.mult, ALU.add)
            return ins

        def mixing(l):
            m = mods[:, 2 * l, :]

            def first_modulation():
                modulation.add(SS_CH, wide(0, 1), 1, 0)

                @block.tensor
                def _(pe):
                    pe.wait_ge(*cond_at.all())
                    modulation.some(pe, SS_CH)
                mod_of(mods[:, 0, 0:16].unsqueeze(2), 0, 1, V("ada_b00")[:, 0:16].unsqueeze(2))
            if l == 0:
                first_modulation()
            whole = norm(xT[:, :, :], hT[:, :, 0:S], V(f"norm_mix{l}"), m[:, 0:8], m[:, 8:16], at=R0)

            @block.vector
            def _(v):
                nc.vector.memset(RAW[:, :, 0:1], 0.0).then_inc(*dve_done.next())

            def reader(b, n):
                src = b[:, :].rearrange("p (f t) -> p f t", f=2)
                if n < SHIFT_T // 2:
                    return act(RAW[:, 2 * n:2 * n + 2, 1:S + 1], src, ACT.Copy)
                m = 2 * n - SHIFT_T
                return act(REST[:, m:m + 2, :], src, ACT.Sigmoid if m >= 6 else ACT.Copy)
            e0 = evac.count
            project(IN_CH, hT[:, :, 0:S], KD, block.scalar, None, reader, tiles=whole)

            @block.vector
            def _(v):
                v.wait_ge(*dve_done.all())
                for j in range(SHIFT_T):
                    v.wait_ge(evac.handle, e0 + j // 2 + 1)
                    tt(SH[:, j, :], RAW[:, j, 0:S], RAW[:, j, 1:S + 1], ALU.subtract)\
                        .then_inc(*dve_done.next())
                    if j:
                        v.wait_ge(dve_done.handle, dve_done.count - 1)
                        stt(SH[:, j - 1, :], SH[:, j - 1, :], col(f"mu{l}", j - 1),
                            RAW[:, j - 1, 1:S + 1], ALU.mult, ALU.add).then_inc(*dve_done.next())
                v.wait_ge(*dve_done.all())
                j = SHIFT_T - 1
                link(stt(SH[:, j, :], SH[:, j, :], col(f"mu{l}", j), RAW[:, j, 1:S + 1],
                         ALU.mult, ALU.add))
            tap(f"sh{l}", SH)
            tap(f"rest{l}", REST)
            rwkv(l)
            mla(l)

            @block.vector
            def _(v):
                v.wait_ge(*evac.all())
                for j in range(4):
                    tt(GA[:, 2 * j:2 * j + 2, :], GA[:, 2 * j:2 * j + 2, :], GB[:, 2 * j:2 * j + 2, :],
                       ALU.add).then_inc(*dve_done.next())
            project(WO_CH, GA, KD, block.vector, None, lambda b, n: add_residual(b, n, m[:, 16:24]))
            tap(f"x{l}", xT[:, :, :])
            f = mods[:, 2 * l + 1, :]
            return norm(xT[:, :, :], hT[:, :, 0:S], V(f"norm_ffn{l}"), f[:, 0:8], f[:, 8:16], at=R0)

        def rwkv(l):
            r, k, v_, wa, pg = SH[:, 0:4, :], SH[:, 4:8, :], SH[:, 8:12, :], SH[:, 12, :], SH[:, 13, :]
            decay, iclr, gate, kk, P, aT, bT, kT, rT, bonus = [slot(n) for n in range(10)]
            t0, t1 = carve(0, [4, S]), carve(1024, [4, S])
            Atok, Btok, Ktok, Vtok = [slot(n, (2, RW)) for n in (0, 1, 3, 4)]
            PC = tiny[:, 16:32].rearrange("p (a b) -> p a b", a=4)

            modulation.add(ADA_CH - SS_CH, wide(0, 1), 1, 0)
            modulation.add(ADA_CH, wide(0, 1), 1, 8)
            modulation.add(SS_CH, *((wide(0, 1), 1) if l == 0 else (wide(1, 2), 2)), 32)

            @block.scalar
            def _(a):
                a.wait_ge(*dve_done.all())
                act(wa[0:64, :], wa[0:64, :], ACT.Tanh).then_inc(*act_done.next())
                act(pg, pg, ACT.Sigmoid).then_inc(*act_done.next())

            @block.tensor
            def _(pe):
                pe.wait_ge(*act_done.all())
                pe.wait_ge(*evac.all())
                w = take(pe)
                for j in range(RT):
                    at = RW + j * 128
                    mm(b2[j // 2][:, j % 2, :], w[0:64, at:at + 128], wa[0:64, :])
                for j in range(RT):
                    at = RW + j * 128
                    mm(b2[2 + j // 2][:, j % 2, :], w[64:128, at:at + 128], wa[64:128, :])
                for j in range(RT):
                    last = mm(b2[4 + j // 2][:, j % 2, :], w[:, j * 128:j * 128 + 128], pg)
                last.then_inc(*used.next())

            @block.scalar
            def _(a):
                a.wait_ge(*used.all())
                for j in range(RT):
                    act(iclr[:, j, :], b2[2 + j // 2][:, j % 2, :], ACT.Sigmoid, bias=col(f"a0{l}", j))\
                        .then_inc(*act_done.next())
                for j in range(RT):
                    act(decay[:, j, :], b2[j // 2][:, j % 2, :], ACT.Sigmoid, bias=col(f"w0{l}", j))\
                        .then_inc(*act_done.next())
                for j in range(2):
                    act(gate[:, 2 * j:2 * j + 2, :], b2[4 + j], ACT.Copy).then_inc(*act_done.next())
                a.wait_ge(*act_done.all())
                act(decay, decay, ACT.Exp, scale=-DECAY_SCALE).then_inc(*act_done.next())

            @block.vector
            def _(v):
                for j in range(RT):
                    ts(kk[:, j, :], k[:, j, :], col(f"k_k{l}", j), None, ALU.mult)\
                        .then_inc(*dve_done.next())
                v.wait_ge(*dve_done.all())
                link(tt(t0, kk, kk, ALU.mult))

            @block.tensor
            def _(pe):
                modulation.some(pe, 3)
                pe.wait_ge(*act_done.all())
            head_sums(t0, 0)
            roots(t1, 0, 1.0, C("eps")[:, 1:2])

            @block.vector
            def _(v):
                link(tt(kk, kk, t1, ALU.mult))
                for j in range(RT):
                    ts(t0[:, j, :], iclr[:, j, :], -1.0, col(f"k_a{l}", j), ALU.add, ALU.mult)\
                        .then_inc(*dve_done.next())
                v.wait_ge(*dve_done.all())
                link(stt(k, t0, 1.0, k, ALU.add, ALU.mult))
                for j in range(RT):
                    stt(t0[:, j, :], r[:, j, :], col(f"r_k{l}", j), k[:, j, :], ALU.mult, ALU.mult)\
                        .then_inc(*dve_done.next())
            fill(4)
            head_sums(t0, 2)
            start = over(C("start"), RT)
            scanned = None

            def ch(ap):
                return ap.rearrange("p a (c t) -> p (a c) t", t=CHUNK)

            @block.gpsimd
            def _(g):
                g.wait_ge(*dve_done.all())
                nc.gpsimd.tensor_tensor(bT, kk, iclr, ALU.mult).then_inc(*pool_done.next())

            @block.vector
            def _(v):
                nonlocal scanned
                v.wait_ge(*pe_done.all())
                for j in range(2):
                    tt(bonus[:, 2 * j:2 * j + 2, :], b2[2 + j], v_[:, 2 * j:2 * j + 2, :], ALU.mult)\
                        .then_inc(*dve_done.next())
                link(tt(t0, decay, start, ALU.mult))
                link(tt(t1, decay, t0, ALU.subtract))
                link(nc.vector.tensor_tensor_scan(flat(P), flat(t1), flat(t0), 0.0, ALU.mult, ALU.add))
                scanned = dve_done.all()
                link(cp(PC, P.rearrange("p a (c t) -> p a c t", t=CHUNK)[:, :, :, CHUNK - 1]))
                link(nc.vector.memset(ch(t0)[:, :, 0:1], 1.0))
                link(cp(ch(t0)[:, :, 1:CHUNK], ch(P)[:, :, 0:CHUNK - 1]))

            @block.scalar
            def _(a):
                a.wait_ge(*scanned)
                alink(act(t1, P, ACT.Ln))
                act(t1, t1, ACT.Exp, scale=-1.0).then_inc(*act_done.next())
            scaled = dve_done.all()

            @block.gpsimd
            def _(g):
                g.wait_ge(*scaled)
                nc.gpsimd.tensor_tensor(rT, r, P, ALU.mult).then_inc(*pool_done.next())

            @block.vector
            def _(v):
                stt(aT, kk, -1.0, t0, ALU.mult, ALU.mult).then_inc(*dve_done.next())
                v.wait_ge(pool_done.handle, pool_done.count - 1)
                v.wait_ge(*act_done.all())
                tt(bT, bT, t1, ALU.mult).then_inc(*dve_done.next())
                tt(kT, k, t1, ALU.mult).then_inc(*dve_done.next())
            fill(4)
            jobs = [(dst, src, t) for dst, src in ((Vtok, v_), (Atok, aT), (Btok, bT), (Ktok, kT))
                    for t in range(2)]
            e0 = evac.count
            p0 = pe_done.count
            d0 = dve_done.count

            @block.tensor
            def _(pe):
                for n, (dst, src, t) in enumerate(jobs):
                    if n % 2 == 0 and n:
                        pe.wait_ge(dve_done.handle, d0 - 3 + n // 2)
                    if n == 7:
                        pe.wait_ge(evac.handle, e0 + 1)
                    for j in range(RT):
                        last = turn(bank[n % 7][:, j * 128:j * 128 + 128],
                                    src[:, j, t * 128:t * 128 + 128], ident)
                    last.then_inc(*pe_done.next())

            @block.scalar
            def _(a):
                a.wait_ge(dve_done.handle, d0)
                a.wait_ge(*pool_done.all())
                for n, (dst, src, t) in enumerate(jobs):
                    a.wait_ge(pe_done.handle, p0 + n + 1)
                    act(dst[:, t, :], bank[n % 7][:, :], ACT.Copy).then_inc(*evac.next())
            tap(f"aT{l}", aT)

            QT = late[:, 0:1024].rearrange("p (a b) -> p a b", a=4)
            Y0 = late[:, 1024:2048].rearrange("p (a b) -> p a b", a=4)
            Phi = carve(R0 + 10240, [4, 4, 64])
            Psi = carve(R0 + 10240 + 1024, [4, 4, 64])
            at = [512 * n for n in range(7)] + [9232 + 512 * n for n in range(7)] \
                + [R0 + 10240 + 2048 + 512 * n for n in range(2)]
            AT, AkT, RbT, RkT, X, XT, NT, Z = [
                [carve(at[8 * w + n], [4, 128]) for w in range(2)] for n in range(8)]
            R, GH = NT, Z

            def fm(ap, h, tok):
                return ap[HALVES[h % 2], h // 2, tok]

            for T in range(2):
                tok = slice(128 * T, 128 * T + 128)
                heads = [[4 * w + u for u in range(4)] for w in range(2)]
                pe_at, act_at, dve_at = [None, None], [None, None], [None, None]

                for part, pairs in enumerate((((0, bT, aT), (1, aT, bT), (2, kT, aT)),
                                              ((0, bT, rT), (1, kT, rT)))):
                    @block.tensor
                    def _(pe):
                        pe.wait_ge(*evac.all())
                        pe.wait_ge(*dve_done.all())
                        pe.wait_ge(*pool_done.all())
                        for w in range(2):
                            for parity in range(2):
                                for u in (parity, parity + 2):
                                    h = heads[w][u]
                                    for b, x, y in pairs:
                                        last = mm(b4[3 * w + b][:, u, :], fm(x, h, tok), fm(y, h, tok))
                                last.then_inc(*pe_done.next())
                                if parity == 0:
                                    pe.wait_ge(*pe_done.all())
                            pe_at[w] = pe_done.all()
                        modulation.some(pe, 1)

                    @block.vector
                    def _(v):
                        for w in range(2):
                            v.wait_ge(*pe_at[w])
                            c = b4[3 * w:3 * w + 3]
                            if part == 0:
                                tt(AT[w], c[0], over(C("upp"), 4), ALU.mult).then_inc(*dve_done.next())
                                tt(X[w], c[1], over(C("lv1"), 4), ALU.mult).then_inc(*dve_done.next())
                                tt(XT[w], c[0], over(C("lvT1"), 4), ALU.mult).then_inc(*dve_done.next())
                                tt(AkT[w], c[2], over(C("upp"), 4), ALU.mult).then_inc(*dve_done.next())
                                v.wait_ge(*dve_done.all())
                                tt(X[w], X[w], over(ident, 4), ALU.add).then_inc(*dve_done.next())
                                tt(XT[w], XT[w], over(ident, 4), ALU.add).then_inc(*dve_done.next())
                            else:
                                tt(RbT[w], c[0], over(C("uppeq"), 4), ALU.mult)\
                                    .then_inc(*dve_done.next())
                                tt(RkT[w], c[1], over(C("uppeq"), 4), ALU.mult)\
                                    .then_inc(*dve_done.next())
                            dve_at[w] = dve_done.all()
                        v.wait_ge(*dve_done.all())

                nt_at = [None, None]
                for m in LEVELS[1:6]:
                    @block.gpsimd
                    def _(g):
                        if m == 2:
                            g.wait_ge(*dve_done.all())
                        for w in range(2):
                            if m > 2:
                                g.wait_ge(*nx_at[w])
                            nc.gpsimd.tensor_tensor(NT[w], AT[w], over(C(f"lvT{m}"), 4), ALU.mult)\
                                .then_inc(*pool_done.next())
                            nt_at[w] = pool_done.all()
                    nx_at = [None, None]

                    @block.tensor
                    def _(pe):
                        for w in range(2):
                            pe.wait_ge(*nt_at[w])
                            pe.wait_ge(*dve_at[w])
                            for u in range(4):
                                last = mm(b4[3 * w][:, u, :], NT[w][:, u, :], X[w][:, u, :])
                            last.then_inc(*pe_done.next())
                            nx_at[w] = pe_done.all()

                    @block.scalar
                    def _(a):
                        for w in range(2):
                            a.wait_ge(*nx_at[w])
                            act(Z[w], b4[3 * w], ACT.Copy).then_inc(*act_done.next())
                            act_at[w] = act_done.all()

                    @block.tensor
                    def _(pe):
                        for w in range(2):
                            pe.wait_ge(*act_at[w])
                            if m < 32:
                                for u in range(4):
                                    mm(b4[3 * w + 1][:, u, :], XT[w][:, u, :], Z[w][:, u, :])
                            for u in range(4):
                                last = mm(b4[3 * w + 2][:, u, :], Z[w][:, u, :], XT[w][:, u, :])
                            last.then_inc(*pe_done.next())
                            pe_at[w] = pe_done.all()

                    @block.vector
                    def _(v):
                        for w in range(2):
                            v.wait_ge(*pe_at[w])
                            if m < 32:
                                tt(X[w], X[w], b4[3 * w + 1], ALU.add).then_inc(*dve_done.next())
                            tt(XT[w], XT[w], b4[3 * w + 2], ALU.add).then_inc(*dve_done.next())
                            dve_at[w] = dve_done.all()
                        v.wait_ge(*dve_done.all())

                @block.tensor
                def _(pe):
                    for w in range(2):
                        for u, h in enumerate(heads[w]):
                            last = mm(b4[3 * w][:, u, 0:64], AkT[w][:, u, :],
                                      Vtok[:, T, 64 * h:64 * h + 64])
                        last.then_inc(*pe_done.next())
                        pe_at[w] = pe_done.all()

                @block.scalar
                def _(a):
                    for w in range(2):
                        a.wait_ge(*pe_at[w])
                        act(R[w][:, :, 0:64],
                            Atok[:, T, 256 * w:256 * w + 256].rearrange("p (a b) -> p a b", a=4),
                            ACT.Copy).then_inc(*act_done.next())
                        act(R[w][:, :, 64:128], b4[3 * w][:, :, 0:64], ACT.Copy)\
                            .then_inc(*act_done.next())
                        act_at[w] = act_done.all()

                @block.tensor
                def _(pe):
                    for w in range(2):
                        pe.wait_ge(*act_at[w])
                        pe.wait_ge(*dve_at[w])
                        for u in range(4):
                            last = mm(b4[3 * w + 1][:, u, :], XT[w][:, u, :], R[w][:, u, :])
                        last.then_inc(*pe_done.next())
                        pe_at[w] = pe_done.all()

                @block.scalar
                def _(a):
                    for w in range(2):
                        a.wait_ge(*pe_at[w])
                        act(GH[w], b4[3 * w + 1], ACT.Copy).then_inc(*act_done.next())
                        act_at[w] = act_done.all()

                @block.tensor
                def _(pe):
                    for w in range(2):
                        pe.wait_ge(*act_at[w])
                        for u, h in enumerate(heads[w]):
                            half, pr = HALVES[h % 2], u // 2
                            mm(b4[3 * w][half, pr, :], GH[w][:, u, 0:64], RbT[w][:, u, :])
                            mm(b4[3 * w + 1][half, pr, :], GH[w][:, u, 64:128], RbT[w][:, u, :],
                               stop=False)
                            last = mm(b4[3 * w + 1][half, pr, :], Vtok[:, T, 64 * h:64 * h + 64],
                                      RkT[w][:, u, :], start=False)
                        last.then_inc(*pe_done.next())
                        for c in range(2):
                            pe.wait_ge(*pe_done.all())
                            for u, h in enumerate(heads[w]):
                                half, tk = HALVES[h % 2], HALVES[c]
                                at = (u // 2 * 2 + c) * 64
                                hd = slice(64 * h, 64 * h + 64)
                                mm(bank[3 * w + 2][half, at:at + 64], GH[w][tk, u, 0:64],
                                   Btok[tk, T, hd])
                                mm(bank[3 * w + 2][half, 256 + at:256 + at + 64], Btok[tk, T, hd],
                                   GH[w][tk, u, 64:128], stop=False)
                                last = mm(bank[3 * w + 2][half, 256 + at:256 + at + 64],
                                          Ktok[tk, T, hd], Vtok[tk, T, hd], start=False)
                            last.then_inc(*pe_done.next())
                        pe_at[w] = pe_done.all()
                    modulation.some(pe, 1)

                @block.vector
                def _(v):
                    for w in range(2):
                        v.wait_ge(*pe_at[w])
                        pr = slice(2 * w, 2 * w + 2)
                        tt(QT[:, pr, tok], b4[3 * w][:, 0:2, :], rT[:, pr, tok], ALU.add)\
                            .then_inc(*dve_done.next())
                        for q in range(2):
                            phi = bank[3 * w + 2][:, 128 * q:128 * q + 128].rearrange(
                                "p (c b) -> p c b", c=2)
                            tt(Phi[:, 2 * w + q, 2 * T:2 * T + 2, :], phi, over(C("halfident"), 2),
                               ALU.add).then_inc(*dve_done.next())
                            cp(Psi[:, 2 * w + q, 2 * T:2 * T + 2, :],
                               bank[3 * w + 2][:, 256 + 128 * q:384 + 128 * q].rearrange(
                                   "p (c b) -> p c b", c=2)).then_inc(*dve_done.next())
                    v.wait_ge(*dve_done.all())

                @block.scalar
                def _(a):
                    for w in range(2):
                        a.wait_ge(*pe_at[w])
                        act(Y0[:, 2 * w:2 * w + 2, tok], b4[3 * w + 1][:, 0:2, :], ACT.Copy)\
                            .then_inc(*evac.next())

            tap(f"Y0{l}", Y0)

            St = [carve(256 * n, [4, 64]) for n in range(4)]

            def pcb(c):
                return PC[:, :, c].unsqueeze(2).to_broadcast([128, 4, 64])

            @block.vector
            def _(v):
                v.wait_ge(*evac.all())
                link(tt(St[1], Psi[:, :, 0, :], pcb(0), ALU.mult))
            for c in (1, 2):
                @block.tensor
                def _(pe):
                    modulation.some(pe, 1)
                    pe.wait_ge(*dve_done.all())
                    for h in range(HEADS):
                        half = HALVES[h % 2]
                        last = mm(bank[0][half, h // 2 * 64:h // 2 * 64 + 64], Phi[half, h // 2, c, :],
                                  St[c][half, h // 2, :])
                    last.then_inc(*pe_done.next())

                @block.vector
                def _(v):
                    v.wait_ge(*pe_done.all())
                    sb_ = bank[0][:, 0:256].rearrange("p (a b) -> p a b", a=4)
                    link(tt(St[c + 1], sb_, Psi[:, :, c, :], ALU.add))
                    link(tt(St[c + 1], St[c + 1], pcb(c), ALU.mult))

            @block.tensor
            def _(pe):
                pe.wait_ge(*dve_done.all())
                for c in (1, 2, 3):
                    for h in range(HEADS):
                        half, p4 = HALVES[h % 2], h // 2
                        last = mm(b2[1 + p4 // 2][half, p4 % 2, 64 * c:64 * c + 64],
                                  St[c][half, p4, :], QT[half, p4, 64 * c:64 * c + 64])
                last.then_inc(*pe_done.next())

            @block.vector
            def _(v):
                v.wait_ge(*pe_done.all())
                for j in range(2):
                    tt(Y0[:, 2 * j:2 * j + 2, 64:S], Y0[:, 2 * j:2 * j + 2, 64:S],
                       b2[1 + j][:, :, 64:S], ALU.add).then_inc(*dve_done.next())
            tap(f"y{l}", Y0)

            head_sums(Y0, 3)

            @block.vector
            def _(v):
                v.wait_ge(*pe_done.all())
                for j in range(2):
                    yj = Y0[:, 2 * j:2 * j + 2, :]
                    stt(yj, b2[3 + j], -1.0 / 64, yj, ALU.mult, ALU.add).then_inc(*dve_done.next())
                v.wait_ge(*dve_done.all())
                link(tt(t0, Y0, Y0, ALU.mult))
            head_sums(t0, 0)
            fill(len(modulation.todo) - MLA_FILL)
            roots(t1, 0, 1.0 / 64, C("eps")[:, 2:3])

            @block.vector
            def _(v):
                for j in range(RT):
                    stt(Y0[:, j, :], Y0[:, j, :], col(f"lnx_g{l}", j), t1[:, j, :], ALU.mult, ALU.mult)\
                        .then_inc(*dve_done.next())
                v.wait_ge(*dve_done.all())
                for j in range(RT):
                    stt(Y0[:, j, :], Y0[:, j, :], col(f"lnx_b{l}", j), bonus[:, j, :], ALU.add, ALU.add)\
                        .then_inc(*dve_done.next())
                v.wait_ge(*dve_done.all())
                link(tt(Y0, Y0, gate, ALU.mult))

            def out(b, n):
                dst = GA[:, 2 * n:2 * n + 2, :]
                return tt(dst, dst, b[:, :].rearrange("p (f t) -> p f t", f=2), ALU.mult)
            project(OUT_CH, Y0, 4, block.vector, None, out)
            tap(f"ya{l}", GA)

        def mla(l):
            qn, kvn = carve(R0, [3, S]), carve(R0 + 768, [2, S])
            qh = carve(R0 + 1280, [HEADS, S])
            kh = carve(R0 + 1280 + 2048, [HEADS, S])
            Vt = carve(R0 + 1280 + 4096, [2, RW])
            sc = carve(R0 + 1280 + 4096 + 1024, [HEADS, 384])
            free = R0 + 1280 + 4096 + 1024 + 3072
            PT = carve(free, [4, 384])
            oT = carve(0, [4, S])
            t0 = carve(1024, [4, S])
            norm(REST[:, 0:3, :], qn, V(f"q_norm{l}"), n_tiles=3, at=free, b=6)
            norm(REST[:, 3:5, :], kvn, V(f"kv_norm{l}"), n_tiles=2, at=free + 1024, b=6)

            fill(MLA_FILL)
            mod_of(mods[:, 2 * l, 16:24].unsqueeze(2), 0, 1, V(f"ada_b{l}0")[:, 16:24].unsqueeze(2))
            mod_of(mods[:, 2 * l + 1, :].unsqueeze(2), 8, 1, V(f"ada_b{l}1").unsqueeze(2))
            if l == 0:
                mod_of(mods[:, 2, 0:16].unsqueeze(2), 32, 1, V("ada_b10")[:, 0:16].unsqueeze(2))
            else:
                mod_of(mod2[:, 0:16, :], 32, 2, bias2(0, 16))

            e0 = evac.count

            @block.tensor
            def _(pe):
                pe.wait_ge(*dve_done.all())
                pe.wait_ge(*evac.all())
                for g in range(QB_CH):
                    w = take(pe)[:, 0:3 * 384].rearrange("p (k f) -> p k f", k=3)
                    for h in range(4):
                        for k in range(3):
                            last = mm(b2[2 * g + h // 2][0:QK, h % 2, :], w[:, k, QK * h:QK * h + QK],
                                      qn[:, k, :], start=k == 0, stop=k == 2)
                    last.then_inc(*used.next())

            @block.scalar
            def _(a):
                for g in range(QB_CH):
                    a.wait_ge(used.handle, used.count - QB_CH + 1 + g)
                    for j in range(2):
                        act(qh[0:QK, 4 * g + 2 * j:4 * g + 2 * j + 2, :], b2[2 * g + j][0:QK, :, :],
                            ACT.Copy).then_inc(*evac.next())

            @block.tensor
            def _(pe):
                w = take(pe).rearrange("p (k h f) -> p k h f", k=2, h=HEADS)
                for t in range(2):
                    for k in range(2):
                        mm(bank[4 + t][:, :].rearrange("p (h f) -> p h f", h=HEADS),
                           kvn[:, k, 128 * t:128 * t + 128], w[:, k, :, 64:128],
                           start=k == 0, stop=k == 1)
                pe.wait_ge(*evac.all())
                for h in range(HEADS):
                    for k in range(2):
                        last = mm(b2[h // 2][0:64, h % 2, :], w[:, k, h, 0:64], kvn[:, k, :],
                                  start=k == 0, stop=k == 1)
                last.then_inc(*used.next())
                mm(bank[6][64:96, 0:S], C("swap")[64:96, :], REST[64:96, 5, :]).then_inc(*pe_done.next())

            @block.scalar
            def _(a):
                a.wait_ge(*used.all())
                for j in range(4):
                    act(kh[0:64, 2 * j:2 * j + 2, :], b2[j][0:64, :, :], ACT.Copy).then_inc(*evac.next())
                for t in range(2):
                    act(Vt[:, t, :], bank[4 + t][:, :], ACT.Copy).then_inc(*evac.next())

            @block.vector
            def _(v):
                v.wait_ge(*pe_done.all())
                rk = REST[64:96, 5, :]
                link(tt(t0[64:96, 0, :], bank[6][64:96, 0:S], rope[64:96, 1, :], ALU.mult))
                link(tt(rk, rk, rope[64:96, 0, :], ALU.mult))
                link(tt(rk, rk, t0[64:96, 0, :], ALU.add))
                link(cp(kh[64:96, :, :], rk.unsqueeze(1).to_broadcast([32, HEADS, S])))

            @block.tensor
            def _(pe):
                pe.wait_ge(*evac.all())
                for j in range(4):
                    last = mm(bank[j][64:96, :], C("swap")[64:96, :], qh[64:96, 2 * j:2 * j + 2, :])
                last.then_inc(*pe_done.next())
            q8 = carve(free, [HEADS, S])

            @block.vector
            def _(v):
                v.wait_ge(*pe_done.all())
                sinb = rope[64:96, 1, :].unsqueeze(1).to_broadcast([32, 2, S])
                for j in range(4):
                    tt(q8[64:96, 2 * j:2 * j + 2, :], b2[j][64:96, :, :], sinb, ALU.mult)\
                        .then_inc(*dve_done.next())
                cosb = rope[64:96, 0, :].unsqueeze(1).to_broadcast([32, HEADS, S])
                link(tt(qh[64:96, :, :], qh[64:96, :, :], cosb, ALU.mult))
                link(tt(qh[64:96, :, :], qh[64:96, :, :], q8[64:96, :, :], ALU.add))
            tap(f"qh{l}", qh)
            tap(f"kh{l}", kh)

            @block.tensor
            def _(pe):
                pe.wait_ge(*dve_done.all())
                for h in range(HEADS):
                    mm(bank[h][:, 0:128], qh[0:QK, h, 0:128], kh[0:QK, h, 0:128])
                    mm(bank[h][:, 128:384], qh[0:QK, h, 128:256], kh[0:QK, h, :])\
                        .then_inc(*pe_done.next())
            spans = ((0, 128), (128, 384))
            mx, sm = tiny[:, 32:48], tiny[:, 48:64]
            max_at = [None] * HEADS

            @block.vector
            def _(v):
                for h in range(HEADS):
                    v.wait_ge(pe_done.handle, pe_done.count - HEADS + 1 + h)
                    link(stt(sc[:, h, :], bank[h][:, 0:384], QK ** -0.5, C("causal"), ALU.mult, ALU.add))
                    for i, (a, b) in enumerate(spans):
                        red(mx[:, 2 * h + i:2 * h + i + 1], sc[:, h, a:b], AX.X, ALU.max, negate=True)\
                            .then_inc(*dve_done.next())
                    max_at[h] = dve_done.all()

            @block.scalar
            def _(a_):
                for h in range(HEADS):
                    a_.wait_ge(*max_at[h])
                    for i, (a, b) in enumerate(spans):
                        n = 2 * h + i
                        act(sc[:, h, a:b], sc[:, h, a:b], ACT.Exp, bias=mx[:, n:n + 1],
                            accum_out=sm[:, n:n + 1]).then_inc(*act_done.next())

            @block.vector
            def _(v):
                v.wait_ge(*act_done.all())
                link(nc.vector.reciprocal(sm, sm))
                for h in range(HEADS):
                    for i, (a, b) in enumerate(spans):
                        n = 2 * h + i
                        ts(sc[:, h, a:b], sc[:, h, a:b], sm[:, n:n + 1], None, ALU.mult)\
                            .then_inc(*dve_done.next())
            d0 = dve_done.count - 2 * HEADS

            for g in range(2):
                @block.tensor
                def _(pe):
                    for u in range(4):
                        h = 4 * g + u
                        pe.wait_ge(dve_done.handle, d0 + 2 * h + 2)
                        for b in range(3):
                            last = turn(bank[u][:, b * 128:b * 128 + 128],
                                        sc[:, h, b * 128:b * 128 + 128], ident)
                        last.then_inc(*pe_done.next())
                e0 = evac.count

                @block.scalar
                def _(a):
                    for u in range(4):
                        a.wait_ge(pe_done.handle, pe_done.count - 3 + u)
                        if g == 0 and u == 0:
                            a.wait_ge(dve_done.handle, d0)
                        act(PT[:, u, :], bank[u][:, 0:384], ACT.Copy).then_inc(*evac.next())

                @block.tensor
                def _(pe):
                    for u in range(4):
                        h = 4 * g + u
                        pe.wait_ge(evac.handle, e0 + u + 1)
                        o = b2[4 + g][HALVES[h % 2], u // 2, :]
                        v0, v1 = [Vt[:, t, 64 * h:64 * h + 64] for t in range(2)]
                        mm(o[:, 0:128], v0, PT[:, u, 0:128])
                        mm(o[:, 128:256], v0, PT[:, u, 128:256], stop=False)
                        last = mm(o[:, 128:256], v1, PT[:, u, 256:384], start=False)
                    last.then_inc(*pe_done.next())

                @block.scalar
                def _(a):
                    a.wait_ge(*pe_done.all())
                    act(oT[:, 2 * g:2 * g + 2, :], b2[4 + g], ACT.Copy).then_inc(*act_done.next())
            tap(f"oT{l}", oT)

            def out(b, n):
                dst = GB[:, 2 * n:2 * n + 2, :]
                return tt(dst, dst, b[:, :].rearrange("p (f t) -> p f t", f=2), ALU.mult)
            project(OUT_CH, oT, 4, block.vector, None, out)

        acc = carve(0, [4, 512])
        G1 = carve(3072, [2, 512])
        gT = carve(4096, [2, 512])

        def dense_pair(chunk, src, first, n_groups, r, at, sems):
            used_, silu_, gated_, acc_ = sems

            def pe_pair(pe):
                for g in range(n_groups):
                    if not first:
                        pe.wait_ge(gated_.handle, r * 2 + (at["gated"] + g - 1))
                    for i in range(2):
                        w = chunk(pe, 2 * g + i).rearrange("p (k f) -> p k f", k=KD)
                        for f in range(2):
                            for k in range(KD):
                                last = mm(b2[2 * g + i][:, f, :], w[:, k, f * 128:f * 128 + 128],
                                          src[:, k, :], start=k == 0, stop=k == KD - 1)
                        last.then_inc(used_.handle, 1)
                for g in range(n_groups):
                    pe.wait_ge(gated_.handle, r * 2 + (at["gated"] + g + 1))
                    if g == 0 and not first:
                        pe.wait_ge(acc_.handle, r + at["acc"])
                    w = chunk(pe, 2 * n_groups + g).rearrange("p (k f) -> p k f", k=2)
                    for k in range(2):
                        for t in range(2):
                            for d in range(2):
                                last = mm(bank[4 + 2 * t + d][:, :],
                                          gT[:, g, k * S + t * 128:k * S + t * 128 + 128],
                                          w[:, k, d * 512:d * 512 + 512],
                                          start=g == 0 and k == 0, stop=g == n_groups - 1 and k == 1)
                    last.then_inc(used_.handle, 1)

            def act_pair(a):
                for g in range(n_groups):
                    a.wait_ge(used_.handle, r * 6 + (at["used"] + 2 * g + 1))
                    if not first:
                        a.wait_ge(gated_.handle, r * 2 + (at["gated"] + g - 1))
                    act(G1[:, g, :], bank[2 * g][:, :], ACT.Silu).then_inc(silu_.handle, 1)

            def dve_pair(v):
                for g in range(n_groups):
                    v.wait_ge(silu_.handle, r * 2 + (at["silu"] + g + 1))
                    v.wait_ge(used_.handle, r * 6 + (at["used"] + 2 * g + 2))
                    tt(gT[:, g, :], G1[:, g, :], bank[2 * g + 1][:, :], ALU.mult)\
                        .then_inc(gated_.handle, 1)
                v.wait_ge(used_.handle, r * 6 + (at["used"] + 3 * n_groups))
                if not first:
                    v.wait_ge(acc_.handle, r + at["acc"])
                for n in range(4):
                    last = stt(acc[:, n, :], bank[4 + n][:, :], weight[:, n // 2:n // 2 + 1],
                               acc[:, n, :], ALU.mult, ALU.add)
                last.then_inc(acc_.handle, 1)
            return pe_pair, act_pair, dve_pair

        def dense_ffn(groups):
            pairs, tail = groups // 2, groups % 2
            at = {"used": used.count, "silu": silu_at.count, "gated": gated.count, "acc": accd.count}

            @block.vector
            def _(v):
                v.wait_ge(*act_done.all())
                nc.vector.memset(acc, 0.0).then_inc(*dve_done.next())
                link(nc.vector.memset(weight[:, :], 1.0))

            @block.tensor
            def _(pe):
                pe.wait_ge(*act_done.all())
                pe.wait_ge(*dve_done.all())
                pe.wait_ge(*evac.all())

            def chunk_at(r):
                def chunk(pe, i):
                    n = at["used"] + i
                    pe.wait_ge(chunk_in[n % RING].handle, (r + (n // RING + 1)) * 16)
                    return ring[:, n % RING, :]
                return chunk
            for lane, engine in enumerate((block.tensor, block.scalar, block.vector)):
                @engine
                def _(eng):
                    def pair(r, first, n_groups):
                        dense_pair(chunk_at(r), hT[:, :, 0:S], first, n_groups, r, at,
                                   (used, silu_at, gated, accd))[lane](eng)
                    pair(0, True, 2)
                    with eng.Fori(1, pairs) as r:
                        pair(r, False, 2)
                    if tail:
                        pair(pairs, False, 1)
            used.next(6 * pairs + 3 * tail)
            silu_at.next(2 * pairs + tail)
            gated.next(2 * pairs + tail)
            accd.next(pairs + tail)

        def add_output(gate):
            @block.tensor
            def _(pe):
                pe.wait_ge(*accd.all())
                pe.wait_ge(*dve_done.all())
                for f in range(KD):
                    for t in range(2):
                        src = acc[:, 2 * t + f // 4, f % 4 * 128:f % 4 * 128 + 128]
                        last = turn(b2[f // 2][:, f % 2, t * 128:t * 128 + 128], src, ident)
                    if f % 2:
                        last.then_inc(*pe_done.next())

            @block.vector
            def _(v):
                for n in range(4):
                    v.wait_ge(pe_done.handle, pe_done.count - 3 + n)
                    add_residual(bank[n], n, gate).then_inc(*dve_done.next())

        B0 = 9100
        E_MAX = E2 + 2
        ybuf = carve(2048, [2, 512])
        xg = carve(5120, [1024])
        htok = carve(6144, [2, D])
        sel, selw = carve(8192, [2, 128]), carve(8448, [2, 128])
        selwT = carve(8704, [256])
        cur = carve(8960, [2, 4])
        route = carve(8968, [E_MAX, 4])

        def logits(n_e, weights, whole):
            @block.tensor
            def _(pe):
                pe.wait_ge(*evac.all())
                for t in range(2):
                    for k in range(KD):
                        if t == 0:
                            pe.wait_ge(act_done.handle, whole + k + 1)
                        last = mm(bank[t][:, 0:n_e], hT[:, k, t * 128:t * 128 + 128],
                                  weights[:, k * n_e:k * n_e + n_e], start=k == 0, stop=k == KD - 1)
                last.then_inc(*pe_done.next())

        m8, idx = carve(B0 + 32, [8]), carve(B0 + 40, [8])

        def one_hot_pair(val, hot0, hot1, n):
            iota = C("iota")[:, 0:n]
            link(nc.vector.max(m8, val))
            link(nc.vector.max_index(i8u[:, :], m8, val))
            link(cp(idx, i8u[:, :]))
            link(ts(hot0, iota, idx[:, 0:1], None, ALU.is_equal))
            link(ts(hot1, iota, idx[:, 1:2], None, ALU.is_equal))

        def route_top2(whole):
            lg = carve(B0, [2, E1])
            h0, h1 = carve(B0 + 48, [E1]), carve(B0 + 64, [E1])
            ex = carve(B0 + 80, [2])
            logits(E1, V("router_w"), whole)
            for t in range(2):
                @block.vector
                def _(v):
                    v.wait_ge(*pe_done.all())
                    link(tt(lg[:, t, :], bank[t][:, 0:E1], V("router_b"), ALU.add))
                    one_hot_pair(lg[:, t, :], h0, h1, E1)
                    link(ts(ex, m8[:, 0:2], m8[:, 0:1], None, ALU.subtract))

                @block.scalar
                def _(a):
                    a.wait_ge(*dve_done.all())
                    act(ex, ex, ACT.Exp).then_inc(*act_done.next())

                @block.vector
                def _(v):
                    v.wait_ge(*act_done.all())
                    link(tt(m8[:, 2:3], ex[:, 0:1], ex[:, 1:2], ALU.add))
                    link(nc.vector.reciprocal(m8[:, 2:3], m8[:, 2:3]))
                    link(ts(ex, ex, m8[:, 2:3], None, ALU.mult))
                    link(ts(h0, h0, ex[:, 0:1], None, ALU.mult))
                    link(stt(comb[:, t, 0:E1], h1, ex[:, 1:2], h0, ALU.mult, ALU.add))

        def route_grouped(whole):
            pr, sl = carve(B0, [E2]), carve(B0 + 16, [E2])
            h0, h1 = carve(B0 + 48, [E2]), carve(B0 + 64, [E2])
            gp, gs = carve(B0 + 80, [8]), carve(B0 + 96, [8])
            m1, n1, m2, n2 = [carve(B0 + 112 + 4 * n, [4]) for n in range(4)]
            logits(E2, V("router_w_2"), whole)
            for t in range(2):
                lg = bank[t][:, 0:E2]

                @block.vector
                def _(v):
                    v.wait_ge(*pe_done.all())
                    link(red(gp[:, 0:1], lg, AX.X, ALU.max))
                    link(ts(pr, lg, gp[:, 0:1], None, ALU.subtract))

                @block.scalar
                def _(a):
                    a.wait_ge(*dve_done.all())
                    act(pr, pr, ACT.Exp, accum_out=gp[:, 1:2]).then_inc(*act_done.next())

                @block.vector
                def _(v):
                    v.wait_ge(*act_done.all())
                    e = sl.rearrange("p (g e) -> p e g", g=4)
                    link(nc.vector.reciprocal(gp[:, 1:2], gp[:, 1:2]))
                    link(ts(pr, pr, gp[:, 1:2], None, ALU.mult))
                    link(tt(sl, pr, V("router_b_2"), ALU.add))
                    link(tt(m1, e[:, 0], e[:, 1], ALU.max))
                    link(tt(n1, e[:, 0], e[:, 1], ALU.min))
                    link(tt(m2, e[:, 2], e[:, 3], ALU.max))
                    link(tt(n2, e[:, 2], e[:, 3], ALU.min))
                    link(nc.vector.memset(gs, -3e38))
                    link(tt(gs[:, 0:4], m1, m2, ALU.add))
                    link(tt(n1, m1, n1, ALU.add))
                    link(tt(n2, m2, n2, ALU.add))
                    link(tt(gs[:, 0:4], gs[:, 0:4], n1, ALU.max))
                    link(tt(gs[:, 0:4], gs[:, 0:4], n2, ALU.max))
                    link(nc.vector.max(m8, gs))
                    link(nc.vector.max_index(i8u[:, :], m8, gs))
                    link(cp(idx, i8u[:, :]))
                    link(ts(h0, C("group"), idx[:, 0:1], None, ALU.is_equal))
                    link(ts(h0, h0, -1.0, 1e30, ALU.add, ALU.mult))
                    link(tt(sl, sl, h0, ALU.add))
                    one_hot_pair(sl, h0, h1, E2)
                    link(tt(h0, h0, h1, ALU.add))
                    link(tt(h0, h0, pr, ALU.mult))
                    link(red(gp[:, 0:1], h0, AX.X, ALU.add))
                    link(nc.vector.reciprocal(gp[:, 0:1], gp[:, 0:1]))
                    link(ts(comb[:, t, :], h0, gp[:, 0:1], None, ALU.mult))

        cur_at, sel_at = signal("picked"), signal("selections_ready")
        gathered, xg_at = signal("gathered"), signal("xg_ready")
        turned, selwT_at = signal("selection_turned"), signal("selwT_ready")
        y_at, scattered = signal("y_added"), signal("scattered")
        f_in, f_used, f_silu = signal("f_chunks_in"), signal("f_used"), signal("f_silu_at")
        f_gated, f_acc, f_weight = signal("f_gated"), signal("f_accumulated"), signal("f_weight_at")

        def moe(E, groups, SL, J, stream_at):
            P, R, W = groups // 2, E // J, J * SL
            assert P == 1 or J == 1
            ind, pos = carve(B0 + 160, [2, E]), carve(B0 + 200, [2, E])
            over_, mxc = carve(B0 + 240, [2, E]), carve(B0 + 280, [1])

            @block.tensor
            def _(pe):
                for t in range(2):
                    for k in range(KD):
                        last = turn(bank[2 + 2 * t + k // 4][:, k % 4 * 128:k % 4 * 128 + 128],
                                    hT[:, k, t * 128:t * 128 + 128], ident)
                    last.then_inc(*pe_done.next())

            @block.scalar
            def _(a):
                for t in range(2):
                    a.wait_ge(pe_done.handle, pe_done.count - 1 + t)
                    for d in range(2):
                        act(htok[:, t, d * 512:d * 512 + 512], bank[2 + 2 * t + d][:, :], ACT.Copy)\
                            .then_inc(*evac.next())

            @block.vector
            def _(v):
                nc.vector.memset(acc, 0.0).then_inc(*y_at.next())
                nc.vector.memset(route, -1.0).then_inc(*dve_done.next())
                nc.vector.memset(selw, 0.0).then_inc(*dve_done.next())
                nc.vector.memset(gT, 0.0).then_inc(*dve_done.next())
                link(ts(ind, comb[:, :, 0:E], 0.0, None, ALU.is_gt))

            @block.tensor
            def _(pe):
                pe.wait_ge(*dve_done.all())
                mm(bank[0][:, 0:E], C("tri"), ind[:, 0, :])
                mm(bank[0][:, E:2 * E], C("tri"), ind[:, 1, :], stop=False)
                mm(bank[0][:, E:2 * E], C("ones"), ind[:, 0, :], start=False)
                for t in range(2):
                    last = mm(bank[1][:, 0:E], C("ones"), ind[:, t, :], start=t == 0, stop=t == 1)
                last.then_inc(*pe_done.next())

            @block.vector
            def _(v):
                v.wait_ge(*pe_done.all())
                cnt = bank[0][:, 0:2 * E].rearrange("p (t e) -> p t e", t=2)
                link(tt(pos, cnt, ind, ALU.mult))
                rt = route[:, 0:E, :].rearrange("p e (w t) -> p w t e", w=2)
                link(ts(rt[:, 0], pos, -1.0, None, ALU.add))
                link(cp(rt[:, 1], comb[:, :, 0:E]))
                link(ts(over_, pos, float(SL), None, ALU.is_gt))
                link(tt(comb[:, :, 0:E], comb[:, :, 0:E], over_, ALU.mult))
                link(red(mxc, bank[1][:, 0:E], AX.X, ALU.max))
                link(ts(mxc, mxc, float(SL), None, ALU.is_gt))
                link(cp(flag[0:1, 0:1], mxc[0:1, :]))
            flag_at = dve_done.all()
            tap(f"route{E}", route)

            at = {n: s.count for n, s in (
                ("used", used), ("silu", silu_at), ("gated", gated), ("acc", accd), ("cur", cur_at),
                ("sel", sel_at), ("gathered", gathered), ("xg", xg_at), ("turned", turned),
                ("selwT", selwT_at), ("y", y_at), ("scattered", scattered))}
            assert at["used"] % RING == 0 and at["acc"] >= 2 and at["gated"] >= 2 and at["y"] >= 1

            def select(v, e, first):
                if not first:
                    v.wait_ge(sel_at.handle, e + at["sel"])
                cp(cur[:, 0:J, :], route[:, bass.ds(e * J, J), :]).then_inc(cur_at.handle, 1)
                if not first:
                    v.wait_ge(gathered.handle, e + at["gathered"])
                    v.wait_ge(turned.handle, e + at["turned"])
                v.wait_ge(cur_at.handle, e + (at["cur"] + 1))
                for j in range(J):
                    for t in range(2):
                        ts(sel[:, t, j * SL:j * SL + SL], C("slots")[:, 0:SL], cur[:, j, t:t + 1], None,
                           ALU.is_equal)
                        last = ts(selw[:, t, j * SL:j * SL + SL], C("slots")[:, 0:SL],
                                  cur[:, j, t:t + 1], cur[:, j, 2 + t:3 + t], ALU.is_equal, ALU.mult)
                last.then_inc(sel_at.handle, 1)

            def gather(pe, e, first):
                pe.wait_ge(sel_at.handle, e + (at["sel"] + 1))
                if not first:
                    pe.wait_ge(selwT_at.handle, e + at["selwT"])
                for k in range(KD):
                    for t in range(2):
                        last = mm(b4[6 + k // 4][:, k % 4, 0:W], htok[:, t, k * 128:k * 128 + 128],
                                  sel[:, t, 0:W], start=t == 0, stop=t == 1)
                last.then_inc(gathered.handle, 1)

            def turn_selection(pe, e):
                pe.wait_ge(xg_at.handle, e + (at["xg"] + 1))
                for t in range(2):
                    last = turn(bank[6][:, t * 128:t * 128 + 128], selw[:, t, :], ident)
                last.then_inc(turned.handle, 1)

            def scatter(pe, e):
                pe.wait_ge(y_at.handle, e * P + (at["y"] + P))
                for t in range(2):
                    for d in range(2):
                        last = mm(bank[2 * t + d][:, :], selwT[:, t * 128:t * 128 + 128], ybuf[:, d, :])
                    last.then_inc(scattered.handle, 1)

            def gathered_out(a, e):
                a.wait_ge(gathered.handle, e + (at["gathered"] + 1))
                for n in range(2):
                    last = act(xs[:, 4 * n:4 * n + 4, 0:W], b4[6 + n][:, :, 0:W], ACT.Copy)
                last.then_inc(xg_at.handle, 1)

            def turned_out(a, e):
                a.wait_ge(turned.handle, e + (at["turned"] + 1))
                act(selwT, bank[6][:, 0:256], ACT.Copy).then_inc(selwT_at.handle, 1)

            def add_up(v, e):
                v.wait_ge(accd.handle, e * 2 + at["acc"])
                for t in range(2):
                    v.wait_ge(scattered.handle, e * 2 + (at["scattered"] + t + 1))
                    for n in (2 * t, 2 * t + 1):
                        last = tt(acc[:, n, :], acc[:, n, :], bank[n][:, :], ALU.add)
                    last.then_inc(accd.handle, 1)

            xs = xg.rearrange("p (k s) -> p k s", k=KD)

            def slots_of(ap, j):
                return ap[:, :, j * SL:j * SL + SL]

            def up(pe, w, b, j):
                w = w.rearrange("p (k f) -> p k f", k=KD)
                for f in range(2):
                    for k in range(KD):
                        last = mm(bank[b][:, f * SL:f * SL + SL], w[:, k, f * 128:f * 128 + 128],
                                  xs[:, k, j * SL:j * SL + SL], start=k == 0, stop=k == KD - 1)
                last.then_inc(used.handle, 1)

            def down(pe, w, n, start, stop):
                w = w.rearrange("p (k f) -> p k f", k=2)
                for k in range(2):
                    for d in range(2):
                        last = mm(bank[4 + d][:, :], hidden[n][:, k, :], w[:, k, d * 512:d * 512 + 512],
                                  start=start and k == 0, stop=stop and k == 1)
                last.then_inc(used.handle, 1)

            hidden = [flat(gT)[:, 256 * n:256 * n + 256].rearrange("p (k s) -> p k s", k=2)
                      for n in range(4)]

            def pe_pair(pe, r, e):
                def chunk(i):
                    pe.wait_ge(chunk_in[i].handle, (r + (at["used"] // RING + 1)) * 16)
                    return ring[:, i, :]
                for g in range(2):
                    if e is None:
                        pe.wait_ge(gated.handle, r * 2 + (at["gated"] + g - 1))
                    else:
                        pe.wait_ge(accd.handle, e * 2 + (at["acc"] + g - 1))
                    for i in range(2):
                        up(pe, chunk(2 * g + i), 2 * g + i, 0)
                for g in range(2):
                    pe.wait_ge(gated.handle, r * 2 + (at["gated"] + g + 1))
                    if g == 0:
                        pe.wait_ge(y_at.handle, r + at["y"])
                    down(pe, chunk(4 + g), g, g == 0, g == 1)

            def act_pair(a, r, e):
                for g in range(2):
                    a.wait_ge(used.handle, r * 6 + (at["used"] + 2 * g + 1))
                    a.wait_ge(gated.handle, r * 2 + (at["gated"] + g - 1))
                    act(G1[:, g, 0:2 * SL], bank[2 * g][:, 0:2 * SL], ACT.Silu)\
                        .then_inc(silu_at.handle, 1)

            def gate_of(v, g, n, j):
                two_tiles = [ap[:, 0:2 * SL].rearrange("p (f s) -> p f s", f=2)
                             for ap in (G1[:, g, :], bank[2 * g + 1])]
                tt(slots_of(hidden[n], j), *two_tiles, ALU.mult).then_inc(gated.handle, 1)

            def dve_pair(v, r, e):
                for g in range(2):
                    v.wait_ge(silu_at.handle, r * 2 + (at["silu"] + g + 1))
                    v.wait_ge(used.handle, r * 6 + (at["used"] + 2 * g + 2))
                    gate_of(v, g, g, 0)
                v.wait_ge(used.handle, r * 6 + (at["used"] + 6))
                v.wait_ge(y_at.handle, r + at["y"])
                for d in range(2):
                    if e is not None:
                        last = cp(ybuf[:, d, :], bank[4 + d][:, :])
                    else:
                        last = tt(ybuf[:, d, :], ybuf[:, d, :], bank[4 + d][:, :], ALU.add)
                last.then_inc(y_at.handle, 1)

            UP, DOWN = (0, 2, 4, 8), (6, 7, 10, 11)

            def pe_two(pe, e):
                def chunk(n):
                    pe.wait_ge(chunk_in[n % RING].handle,
                               (e * 2 + (at["used"] // RING + n // RING + 1)) * 16)
                    return ring[:, n % RING, :]
                for j in range(2):
                    for g in range(2):
                        if j == 1 and g == 1:
                            pe.wait_ge(y_at.handle, e + at["y"])
                            for n in range(2):
                                pe.wait_ge(gated.handle, e * 4 + (at["gated"] + n + 1))
                                down(pe, chunk(DOWN[n]), n, n == 0, False)
                        if j == 0:
                            pe.wait_ge(accd.handle, e * 2 + (at["acc"] + g - 1))
                        else:
                            pe.wait_ge(gated.handle, e * 4 + (at["gated"] + g + 1))
                        for i in range(2):
                            up(pe, chunk(UP[2 * j + g] + i), 2 * g + i, j)
                for n in (2, 3):
                    pe.wait_ge(gated.handle, e * 4 + (at["gated"] + n + 1))
                    down(pe, chunk(DOWN[n]), n, False, n == 3)

            def act_two(a, e):
                for n in range(4):
                    a.wait_ge(used.handle, e * 12 + (at["used"] + UP[n] + 1))
                    a.wait_ge(gated.handle, e * 4 + (at["gated"] + n - 1))
                    act(G1[:, n % 2, 0:2 * SL], bank[2 * (n % 2)][:, 0:2 * SL], ACT.Silu)\
                        .then_inc(silu_at.handle, 1)

            def dve_two(v, e):
                for n in range(4):
                    v.wait_ge(silu_at.handle, e * 4 + (at["silu"] + n + 1))
                    v.wait_ge(used.handle, e * 12 + (at["used"] + UP[n] + 2))
                    gate_of(v, n % 2, n, n // 2)
                v.wait_ge(used.handle, e * 12 + (at["used"] + 12))
                for d in range(2):
                    last = cp(ybuf[:, d, :], bank[4 + d][:, :])
                last.then_inc(y_at.handle, 1)

            def experts(eng, pair, both, e):
                if J == 2:
                    both(eng, e)
                else:
                    pair(eng, e * P, e)
                    with eng.Fori(1, P) as p:
                        pair(eng, e * P + p, None)

            @block.vector
            def _(v):
                v.wait_ge(*dve_done.all())
                select(v, 0, True)
                with v.Fori(0, R) as e:
                    select(v, e + 1, False)
                    experts(v, dve_pair, dve_two, e)
                    add_up(v, e)

            @block.tensor
            def _(pe):
                pe.wait_ge(*evac.all())
                gather(pe, 0, True)
                turn_selection(pe, 0)
                with pe.Fori(0, R) as e:
                    pe.wait_ge(xg_at.handle, e + (at["xg"] + 1))
                    experts(pe, pe_pair, pe_two, e)
                    gather(pe, e + 1, False)
                    scatter(pe, e)
                    turn_selection(pe, e + 1)

            @block.scalar
            def _(a):
                gathered_out(a, 0)
                turned_out(a, 0)
                with a.Fori(0, R) as e:
                    experts(a, act_pair, act_two, e)
                    gathered_out(a, e + 1)
                    turned_out(a, e + 1)
            for s, n in ((used, 6 * E * P), (silu_at, 2 * E * P), (gated, 2 * E * P), (accd, 2 * R),
                         (cur_at, R + 1), (sel_at, R + 1), (gathered, R + 1), (xg_at, R + 1),
                         (turned, R + 1), (selwT_at, R + 1), (y_at, R * P), (scattered, 2 * R)):
                s.next(n)
            overflow(R, J, P, stream_at, flag_at)

        def overflow(R, J, P, stream_at, flag_at):
            fring = carve(10000, [RING, CHUNK_COLS])
            zero = {"used": 0, "silu": 0, "gated": 2, "acc": 1}
            sems = (f_used, f_silu, f_gated, f_acc)

            def chunk(pe, i):
                return fring[:, i, :]

            def source(e, j, p, n):
                if J == 1:
                    return e * (6 * P) + p * 6 + (stream_at + n)
                return e * 12 + (stream_at + ((0, 1, 2, 3, 6, 7), (4, 5, 8, 9, 10, 11))[j][n])

            def pair_of(lane, eng, r):
                dense_pair(chunk, hT[:, :, 0:S], False, 2, r, zero, sems)[lane](eng)

            @block.scalar
            def _(a):
                a.wait_ge(*flag_at)
                a.wait_ge(*accd.all())
                more = a.value_load(flag[0:1, 0:1])
                with a.If(more != 0):
                    with a.Fori(0, R) as e:
                        for j in range(J):
                            with a.Fori(0, P) as p:
                                r = (e * J + j) * P + p
                                a.wait_ge(f_acc.handle, r + 1)
                                for n in range(RING):
                                    src = stream_in[bass.ds(source(e, j, p, n), 1), :, :]
                                    a.dma_start(fring[:, n, :], src.rearrange("a p n -> (a p) n"))\
                                        .then_inc(f_in.handle, 16)
                                pair_of(1, a, r)
                    a.wait_ge(f_weight.handle, R * J + 2)
                    for s in (f_in, f_used, f_silu, f_gated, f_acc):
                        a.sem_clear(s.handle)
                    a.sem_inc(f_weight.handle, 1)

            @block.tensor
            def _(pe):
                pe.wait_ge(*flag_at)
                pe.wait_ge(*accd.all())
                more = pe.value_load(flag[0:1, 0:1])
                with pe.If(more != 0):
                    with pe.Fori(0, R * J * P) as r:
                        pe.wait_ge(f_in.handle, (r + 1) * (16 * RING))
                        pair_of(0, pe, r)
                    pe.sem_inc(f_weight.handle, 1)

            @block.vector
            def _(v):
                v.wait_ge(*flag_at)
                v.wait_ge(*accd.all())
                more = v.value_load(flag[0:1, 0:1])
                with v.If(more != 0):
                    v.sem_inc(f_acc.handle, 1)
                    v.sem_inc(f_gated.handle, 2)
                    with v.Fori(0, R * J) as e:
                        v.wait_ge(f_acc.handle, e * P + 1)
                        cp(weight[:, :].unsqueeze(2), comb[:, :, bass.ds(e, 1)])\
                            .then_inc(f_weight.handle, 1)
                        with v.Fori(0, P) as p:
                            v.wait_ge(f_weight.handle, e + 1)
                            pair_of(2, v, e * P + p)
                    v.wait_ge(f_acc.handle, R * J * P + 1)
                    v.sem_inc(f_weight.handle, 1)
                    v.wait_ge(f_weight.handle, R * J + 3)
                    v.sem_clear(f_weight.handle)
                nc.vector.memset(weight[:, :], 0.0).then_inc(*dve_done.next())

        LC0 = LATE_AT["oddC"][0]

        def LCt(name):
            a, w = LATE_AT[name]
            return A[:, a - LC0:a - LC0 + w]

        def LC3(name):
            return LCt(name).rearrange("p (k n) -> p k n", k=2)

        Z0 = LATE_COLS - LC0
        ZX = carve(Z0, [IN2_T, S])
        ZC = carve(Z0 + IN2_T * S, [12, S])
        W0 = Z0 + 40 * S
        MIX = hT[:, :, 0:S]

        def second_block():
            @block.scalar
            def _(a):
                a.wait_ge(*dve_done.all())
                for dst, src in ((late[:, :], late_in[:, 0:LC0]), (A[:, 0:LATE_COLS - LC0], late_in[:, LC0:]),
                                 (hT[:, :, S:2 * S], ctx_in)):
                    a.dma_start(dst, src).then_inc(*late_at.next(16))
            norm(xT[:, :, :], xT[:, :, :], V("norm_final"), at=W0)

            @block.vector
            def _(v):
                v.wait_ge(*late_at.all())
                link(tt(xT[:, :, :], xT[:, :, :], late[:, :].rearrange("p (k t) -> p k t", k=KD),
                        ALU.add))
            norm(hT[:, :, S:2 * S], hT[:, :, S:2 * S], V("norm1_g_2"), mod2[:, 0:8, 1],
                 mod2[:, 8:16, 1], at=W0, b=6)
            whole = norm(
                xT[:, :, :], hT[:, :, 0:S], V("norm1_g_2"), mod2[:, 0:8, 0], mod2[:, 8:16, 0],
                 at=W0 + 2304)
            c0, e0 = used.count, evac.count
            n_ch = IN2_T // 2

            def both(n):
                return 5 <= n <= 10

            @block.tensor
            def _(pe):
                for n in range(n_ch):
                    w = take(pe).rearrange("p (k f) -> p k f", k=KD)
                    if n >= 4:
                        pe.wait_ge(evac.handle, e0 + n - 3)
                    cols = 2 * S if both(n) else S
                    for f in range(2):
                        for k in range(KD):
                            if n == f == 0:
                                pe.wait_ge(act_done.handle, whole + k + 1)
                            last = mm(bank[n % 4 * 2 + f][:, 0:cols], w[:, k, f * 128:f * 128 + 128],
                                      hT[:, k, 0:cols], start=k == 0, stop=k == KD - 1)
                    last.then_inc(*used.next())

            @block.scalar
            def _(a):
                for n in range(n_ch):
                    a.wait_ge(used.handle, c0 + n + 1)
                    func = ACT.Silu if n in (3, 4, 11, 12) else ACT.Sigmoid if 5 <= n <= 8 else ACT.Copy
                    for f in range(2):
                        b = bank[n % 4 * 2 + f]
                        last = act(ZX[:, 2 * n + f, :], b[:, 0:S], func)
                        if both(n):
                            last = act(ZC[:, 2 * n + f - 10, :], b[:, S:2 * S], func)
                    last.then_inc(*evac.next())
            tap("zx", ZX)
            modulation.add(ADA2_CH - SS_CH, wide(1, 2), 2, 0)
            hyena(e0)
            tap("hy", MIX[:, 0:2, :])
            fourier()
            tap("fn", MIX[:, 6:8, :])
            hgrn()
            tap("hg", MIX[:, 2:6, :])
            project(WO_CH, MIX, KD, block.vector, None,
                    lambda b, n: add_residual(b, n, mod2[:, 16:24, 0]))
            tap("x2", xT[:, :, :])
            route_grouped(norm(xT[:, :, :], hT[:, :, 0:S], V("norm2_g_2"), mod2[:, 24:32, 0],
                               mod2[:, 32:40, 0], at=W0))
            tap("comb2", comb[:, :, :])
            skip(PAD_2)
            moe(E2, F2 // GROUP, 64, 2, STREAM_CH - MOE2_CH)
            add_output(mod2[:, 40:48, 0])
            fin = carve(W0, [KD, S])
            norm(xT[:, :, :], fin, V("final_norm_g_2"), at=W0 + 2048)
            tok = carve(0, [2, D])
            e0 = evac.count

            @block.tensor
            def _(pe):
                pe.wait_ge(*dve_done.all())
                for t in range(2):
                    for f in range(KD):
                        last = turn(bank[2 * t + f // 4][:, f % 4 * 128:f % 4 * 128 + 128],
                                    fin[:, f, t * 128:t * 128 + 128], ident)
                    last.then_inc(*pe_done.next())

            @block.scalar
            def _(a):
                for t in range(2):
                    a.wait_ge(pe_done.handle, pe_done.count - 1 + t)
                    for d in range(2):
                        act(tok[:, t, d * 512:d * 512 + 512], bank[2 * t + d][:, :], ACT.Copy)\
                            .then_inc(*evac.next())

            @block.sync
            def _(sp):
                for t in range(2):
                    sp.wait_ge(evac.handle, e0 + 2 * t + 2)
                    sp.dma_start(fin_out[t * 128:t * 128 + 128, :], tok[:, t, :]).then_inc(*out_at.next(16))
                sp.wait_ge(*out_at.all())

        def hyena(e0):
            U = carve(W0, [6, S])
            h1, tn = carve(W0 + 1536, [S]), carve(W0 + 1792, [S])
            h2 = carve(W0 + 2048, [S])
            filt = carve(W0 + 2304, [2, 1024])
            hs, hd = carve(W0 + 4352, [2, S]), carve(W0 + 4864, [2, S])
            Kr, Ki = carve(W0 + 5376, [2, S]), carve(W0 + 5888, [2, S])
            vt = carve(W0 + 6400, [2, S])
            Yr, Yi = carve(W0 + 6912, [2, S]), carve(W0 + 7424, [2, S])
            p1 = carve(W0 + 7936, [2, S])

            @block.vector
            def _(v):
                v.wait_ge(evac.handle, e0 + 3)
                for j in range(6):
                    z = ZX[:, j, :]
                    link(ts(U[:, j, :], z, col("conv_w1", j), col("conv_b", j), ALU.mult, ALU.add))
                    link(stt(U[:, j, 1:S], z[:, 0:S - 1], col("conv_w0", j), U[:, j, 1:S],
                             ALU.mult, ALU.add))
                    link(stt(U[:, j, 0:S - 1], z[:, 1:S], col("conv_w2", j), U[:, j, 0:S - 1],
                             ALU.mult, ALU.add))

            @block.tensor
            def _(pe):
                pe.wait_ge(*evac.all())
                mm(bank[0][0:64, 0:S], V("filt_w1")[0:33, :], LCt("z")[0:33, :]).then_inc(*pe_done.next())
                modulation.some(pe, 1)
            for n, (bias, dst) in enumerate((("filt_b1", h1), ("filt_b2", h2))):
                @block.vector
                def _(v):
                    v.wait_ge(*pe_done.all())
                    link(ts(p1[0:64, 0, :], bank[0][0:64, 0:S], V(bias)[0:64, :],
                            V("filt_freq")[0:64, :], ALU.add, ALU.mult))
                    wrap(dst[0:64, :], p1[0:64, 0, :], tn[0:64, :], 0.0)

                @block.scalar
                def _(a):
                    a.wait_ge(*dve_done.all())
                    act(dst[0:64, :], dst[0:64, :], ACT.Sin).then_inc(*act_done.next())
                if n == 0:
                    @block.tensor
                    def _(pe):
                        pe.wait_ge(*act_done.all())
                        mm(bank[0][0:64, 0:S], V("filt_w2")[0:64, :], h1[0:64, :])\
                            .then_inc(*pe_done.next())
                        modulation.some(pe, 1)

            @block.tensor
            def _(pe):
                pe.wait_ge(*act_done.all())
                for t in range(2):
                    for d in range(2):
                        last = mm(bank[2 * t + d][:, :], h2[0:64, t * 128:t * 128 + 128],
                                  V("filt_w3")[0:64, d * 512:d * 512 + 512])
                last.then_inc(*pe_done.next())

            @block.vector
            def _(v):
                v.wait_ge(*pe_done.all())
                for t in range(2):
                    for d in range(2):
                        tt(filt[:, t, d * 512:d * 512 + 512].rearrange("p (a b) -> p a b", a=2),
                           b2[2 * t + d], over(LC3("hdecay")[:, t, :], 2), ALU.mult)\
                            .then_inc(*dve_done.next())
                v.wait_ge(*dve_done.all())
                link(nc.vector.memset(filt[0:1, 0, S:2 * S], 0.0))
                link(nc.vector.memset(filt[0:1, 0, 3 * S:4 * S], 0.0))
            value = U[:, 0:2, :]
            for o in range(2):
                hf, hb = filt[:, :, 2 * o * S:2 * o * S + S], filt[:, :, (2 * o + 1) * S:(2 * o + 2) * S]

                @block.vector
                def _(v):
                    tt(hs, hf, hb, ALU.add).then_inc(*dve_done.next())
                    tt(hd, hb, hf, ALU.subtract).then_inc(*dve_done.next())

                @block.tensor
                def _(pe):
                    modulation.some(pe, 1)
                    pe.wait_ge(*dve_done.all())
                    for t in range(2):
                        for j in range(2):
                            last = turn(b2[4][:, t, j * 128:j * 128 + 128],
                                        value[:, j, t * 128:t * 128 + 128], ident)
                    last.then_inc(*pe_done.next())

                @block.scalar
                def _(a):
                    a.wait_ge(*pe_done.all())
                    act(vt, b2[4], ACT.Copy).then_inc(*act_done.next())

                @block.tensor
                def _(pe):
                    for b, src, name in ((0, hs, "oddCT"), (1, hd, "oddST"), (2, vt, "oddCT"),
                                         (3, vt, "oddST")):
                        if b == 2:
                            pe.wait_ge(*act_done.all())
                        for n in range(2):
                            for k in range(2):
                                last = mm(b2[b][:, n, :], LC3(name)[:, k, n * 128:n * 128 + 128],
                                          src[:, k, :], start=k == 0, stop=k == 1)
                        if b == 1:
                            last.then_inc(*pe_done.next())
                    last.then_inc(*pe_done.next())

                @block.scalar
                def _(a):
                    a.wait_ge(pe_done.handle, pe_done.count - 1)
                    act(Kr, b2[0], ACT.Copy).then_inc(*act_done.next())
                    act(Ki, b2[1], ACT.Copy).then_inc(*act_done.next())

                @block.vector
                def _(v):
                    v.wait_ge(*act_done.all())
                    v.wait_ge(*pe_done.all())
                    tt(Yr, b2[2], Kr, ALU.mult).then_inc(*dve_done.next())
                    link(tt(p1, b2[3], Ki, ALU.mult))
                    link(tt(Yr, Yr, p1, ALU.add))
                    tt(Yi, b2[3], Kr, ALU.mult).then_inc(*dve_done.next())
                    link(tt(p1, b2[2], Ki, ALU.mult))
                    tt(Yi, Yi, p1, ALU.subtract).then_inc(*dve_done.next())

                @block.tensor
                def _(pe):
                    modulation.some(pe, 1)
                    pe.wait_ge(*dve_done.all())
                    for j in range(2):
                        for i, (y, m) in enumerate(((Yr, LC3("oddC")), (Yi, LC3("oddS")))):
                            for k in range(2):
                                last = mm(b2[5][:, j, :], y[:, k, j * 128:j * 128 + 128], m[:, k, :],
                                          start=i == 0 and k == 0, stop=i == 1 and k == 1)
                    last.then_inc(*pe_done.next())

                @block.vector
                def _(v):
                    for j in range(2):
                        ts(value[:, j, :], value[:, j, :], col(f"hy_bias{o}", j), None, ALU.mult)\
                            .then_inc(*dve_done.next())
                    v.wait_ge(*dve_done.all())
                    v.wait_ge(*pe_done.all())
                    link(stt(value, b2[5], 1.0 / 256, value, ALU.mult, ALU.add))
                    link(tt(value, value, U[:, 2 * o + 2:2 * o + 4, :], ALU.mult))
            norm(value, MIX[:, 0:2, :], V("hy_norm_g_2"), n_tiles=2, at=W0 + 4352)

        def fourier():
            z = ZX[:, 26:28, :]
            zc, zs = carve(W0, [2, S]), carve(W0 + 512, [2, S])
            y, o = carve(W0 + 1024, [2, S]), carve(W0 + 1536, [2, S])

            @block.tensor
            def _(pe):
                modulation.some(pe, 1)
                pe.wait_ge(*dve_done.all())
                for n, g in enumerate(("gC", "gS")):
                    for t in range(2):
                        for j in range(2):
                            last = mm(b2[1 + n][:, t, j * 128:j * 128 + 128],
                                      z[:, j, t * 128:t * 128 + 128], LCt(g))
                last.then_inc(*pe_done.next())

            @block.scalar
            def _(a):
                a.wait_ge(*pe_done.all())
                act(zc, b2[1], ACT.Copy).then_inc(*act_done.next())
                act(zs, b2[2], ACT.Copy, scale=-1.0).then_inc(*act_done.next())

            @block.tensor
            def _(pe):
                pe.wait_ge(*act_done.all())
                for j in range(2):
                    for i, (a, m) in enumerate(((zc, LC3("fC")), (zs, LC3("fS")))):
                        for k in range(2):
                            last = mm(b2[3][:, j, :], a[:, k, j * 128:j * 128 + 128], m[:, k, :],
                                      start=i == 0 and k == 0, stop=i == 1 and k == 1)
                last.then_inc(*pe_done.next())

            @block.scalar
            def _(a):
                a.wait_ge(*pe_done.all())
                act(y, b2[3], ACT.Copy).then_inc(*act_done.next())

            @block.tensor
            def _(pe):
                pe.wait_ge(*act_done.all())
                for j in range(2):
                    for h in HALVES:
                        last = mm(b2[4][h, j, :], V("fn_w")[h, 64 * j:64 * j + 64], y[h, j, :])
                last.then_inc(*pe_done.next())

            @block.vector
            def _(v):
                v.wait_ge(*pe_done.all())
                for j in range(2):
                    ts(o[:, j, :], b2[4][:, j, :], col("fn_b_2", j), None, ALU.add)\
                        .then_inc(*dve_done.next())
            norm(o, MIX[:, 6:8, :], V("fn_norm_g_2"), n_tiles=2, at=W0 + 2048, b=5)

        def hgrn():
            k0, k1, lf0, lf1, b, w0_, w1_, q0, q1, kt0, kt1 = [
                carve(W0 + 1024 * n, [4, S]) for n in range(11)]
            k, lf, wd, qd, kd = (k0, k1), (lf0, lf1), (w0_, w1_), (q0, q1), (kt0, kt1)
            Vx = late[:, 0:1024].rearrange("p (t n) -> p t n", t=2)
            Vc = late[:, 1024:2048].rearrange("p (t n) -> p t n", t=2)
            AT = carve(0, [4, 2, S])
            St = [carve(2048 + 512 * d, [4, 128]) for d in range(2)]
            qf = [carve(3072, [4, S]), carve(Z0, [4, S])]
            q = ZX[:, 6:10, :]
            run_c, run_x = w1_, ZC[:, 0:4, :]
            L0 = W0 + 11264
            lb, oneml = [carve(L0, [4]), carve(L0 + 4, [4])], [carve(L0 + 8, [4]), carve(L0 + 12, [4])]
            tmp = carve(L0 + 16, [4])
            last_ = b[:, :, S - 1:S].to_broadcast([128, 4, S])

            @block.tensor
            def _(pe):
                pe.wait_ge(*dve_done.all())
                for n, src in ((0, ZX[:, 18:22, :]), (2, ZC[:, 8:12, :])):
                    for t in range(2):
                        for j in range(4):
                            last = turn(bank[n + t][:, j * 128:j * 128 + 128],
                                        src[:, j, t * 128:t * 128 + 128], ident)
                last.then_inc(*pe_done.next())

            @block.vector
            def _(v):
                for d, name in enumerate(("lb_f", "lb_b")):
                    link(tt(lb[d], V(name), V(name), ALU.subtract))

            @block.scalar
            def _(a):
                a.wait_ge(*dve_done.all())
                for d in range(2):
                    act(lb[d], lb[d], ACT.Exp).then_inc(*act_done.next())

            @block.vector
            def _(v):
                v.wait_ge(*act_done.all())
                for d in range(2):
                    link(nc.vector.reciprocal(tmp, lb[d]))
                    link(tt(lb[d], lb[d], tmp, ALU.mult))
                    link(tt(lb[d], lb[d], lb[d], ALU.subtract))
                    link(ts(oneml[d], lb[d], -1.0, 1.0, ALU.mult, ALU.add))
                link(ts(q, q, 128.0 ** -0.5, None, ALU.mult))

            @block.scalar
            def _(a):
                a.wait_ge(*pe_done.all())
                for n, dst in ((0, Vx), (2, Vc)):
                    for t in range(2):
                        act(dst[:, t, :], bank[n + t][:, :], ACT.Copy).then_inc(*act_done.next())

            def gates(f, d):
                @block.vector
                def _(v):
                    for j in range(4):
                        ts(f[:, j, :], f[:, j, :], oneml[d][:, j:j + 1], lb[d][:, j:j + 1],
                           ALU.mult, ALU.add).then_inc(*dve_done.next())
                    v.wait_ge(*dve_done.all())
                    ts(k[d], f, -1.0, 1.0, ALU.mult, ALU.add).then_inc(*dve_done.next())

                @block.scalar
                def _(a):
                    a.wait_ge(*dve_done.all())
                    act(lf[d], f, ACT.Ln).then_inc(*act_done.next())

            def sums(d, name, run):
                link(cp(run, over(LCt(name), 4)))
                link(nc.vector.tensor_tensor_scan(flat(b), flat(run), flat(lf[d]), 0.0,
                                                  ALU.mult, ALU.add))

            for d in range(2):
                gates(ZC[:, 4 * d:4 * d + 4, :], d)

                @block.vector
                def _(v):
                    v.wait_ge(*act_done.all())
                    sums(d, "run256", run_c)
                    if d == 0:
                        link(tt(w0_, last_, b, ALU.subtract))
                    else:
                        link(tt(w0_, b, lf[d], ALU.subtract))

                @block.scalar
                def _(a):
                    a.wait_ge(*dve_done.all())
                    act(w0_, w0_, ACT.Exp).then_inc(*act_done.next())

                @block.vector
                def _(v):
                    v.wait_ge(*act_done.all())
                    tt(kt0, k[d], w0_, ALU.mult).then_inc(*dve_done.next())

                fill(2)

                @block.tensor
                def _(pe):
                    pe.wait_ge(*dve_done.all())
                    for t in range(2):
                        for j in range(4):
                            last = turn(bank[t][:, j * 128:j * 128 + 128],
                                        kt0[:, j, t * 128:t * 128 + 128], ident)
                    last.then_inc(*pe_done.next())
                ktok = flat(q0).rearrange("p (t n) -> p t n", t=2)

                @block.scalar
                def _(a):
                    a.wait_ge(*pe_done.all())
                    for t in range(2):
                        act(ktok[:, t, :], bank[t][:, :], ACT.Copy).then_inc(*act_done.next())

                @block.tensor
                def _(pe):
                    pe.wait_ge(*act_done.all())
                    for j in range(4):
                        for t in range(2):
                            last = mm(b4[2][:, j, :], ktok[:, t, j * 128:j * 128 + 128],
                                      Vc[:, t, j * 128:j * 128 + 128], start=t == 0, stop=t == 1)
                    last.then_inc(*pe_done.next())

                @block.scalar
                def _(a):
                    a.wait_ge(*pe_done.all())
                    act(St[d], b4[2], ACT.Copy).then_inc(*act_done.next())
            tap("St", St[0])
            for d in range(2):
                gates(ZX[:, 10 + 4 * d:14 + 4 * d, :], d)

            steps = [(d, m) for d in range(2) for m in LEVELS + [128]]
            exp_at, q_at, k_at, mm_at = [None] * 16, [None] * 16, [None] * 16, [None] * 16
            sub_at, scores_at = [None] * 16, [None] * 16

            def put(v, i):
                d, m = steps[i]
                v.wait_ge(*mm_at[i])
                if i >= 1:
                    v.wait_ge(*scores_at[i - 1])
                c = b4[2 * (i % 2):2 * (i % 2) + 2]
                if m == 128:
                    a, z = (0, 1) if d == 0 else (1, 0)
                    cp(AT[:, :, a, 128 * z:128 * z + 128], c[0]).then_inc(*dve_done.next())
                    return
                name = C(f"lvT{m}" if d == 0 else f"lv{m}")
                for T in range(2):
                    dst = AT[:, :, T, 128 * T:128 * T + 128]
                    if i == 0:
                        tt(dst, c[T], over(name, 4), ALU.mult).then_inc(*dve_done.next())
                    else:
                        nc.vector.copy_predicated(dst, over(name, 4).bitcast(I32), c[T])\
                            .then_inc(*dve_done.next())
            for i in range(len(steps) + 2):
                @block.vector
                def _(v):
                    if i < len(steps):
                        d, m = steps[i]
                        v.wait_ge(*act_done.all())
                        if m in (1, 64, 128):
                            sums(d, {1: "run64", 64: "run128", 128: "run256"}[m], run_x)
                        w = wd[i % 2]
                        if i >= 2:
                            v.wait_ge(*k_at[i - 2])
                            v.wait_ge(*q_at[i - 2])
                        src = b
                        if d == 1:
                            link(tt(w, b, lf[1], ALU.subtract))
                            src = w

                        def blocks(ap):
                            return flat(ap).rearrange("p (n t) -> p n t", t=2 * m)
                        ref = blocks(b)[:, :, m - 1:m].to_broadcast([128, 512 // m, 2 * m])
                        tt(blocks(w), blocks(src), ref, ALU.subtract).then_inc(*dve_done.next())
                        sub_at[i] = dve_done.all()
                    if 1 <= i <= len(steps):
                        j = i - 1
                        v.wait_ge(*exp_at[j])
                        if j >= 2:
                            v.wait_ge(*mm_at[j - 2])
                        tt(qd[j % 2], q, wd[j % 2], ALU.mult).then_inc(*dve_done.next())
                        q_at[j] = dve_done.all()
                    if i >= 2:
                        put(v, i - 2)
                        scores_at[i - 2] = dve_done.all()
                put_at = dve_done.all()
                if 1 <= i <= len(steps):
                    @block.gpsimd
                    def _(g):
                        j = i - 1
                        g.wait_ge(*exp_at[j])
                        if j >= 2:
                            g.wait_ge(*mm_at[j - 2])
                        nc.gpsimd.tensor_tensor(kd[j % 2], k[steps[j][0]], wd[j % 2], ALU.mult)\
                            .then_inc(*pool_done.next())
                        k_at[j] = pool_done.all()
                if i < len(steps):
                    @block.scalar
                    def _(a):
                        a.wait_ge(*sub_at[i])
                        alink(act(wd[i % 2], wd[i % 2], ACT.Abs))
                        act(wd[i % 2], wd[i % 2], ACT.Exp, scale=-1.0).then_inc(*act_done.next())
                        exp_at[i] = act_done.all()
                if 1 <= i <= len(steps):
                    @block.tensor
                    def _(pe):
                        j = i - 1
                        d, m = steps[j]
                        modulation.some(pe, 1)
                        pe.wait_ge(*q_at[j])
                        pe.wait_ge(*k_at[j])
                        if j == 0:
                            pe.wait_ge(*act_done.all())
                        if j >= 2:
                            pe.wait_ge(*bank_free[j % 2])
                        qt, kt, c = qd[j % 2], kd[j % 2], b4[2 * (j % 2):2 * (j % 2) + 2]
                        if m == 128:
                            a, z = (0, 1) if d == 0 else (1, 0)
                            for h in range(4):
                                last = mm(c[0][:, h, :], kt[:, h, 128 * a:128 * a + 128],
                                          qt[:, h, 128 * z:128 * z + 128])
                        else:
                            for T in range(2):
                                for h in range(4):
                                    last = mm(c[T][:, h, :], kt[:, h, 128 * T:128 * T + 128],
                                              qt[:, h, 128 * T:128 * T + 128])
                        last.then_inc(*pe_done.next())
                        mm_at[j] = pe_done.all()
                if i == 0:
                    bank_free = [None, None]
                bank_free[i % 2] = put_at

                if i < len(steps) and steps[i][1] == 128:
                    d = steps[i][0]

                    @block.vector
                    def _(v):
                        if d == 0:
                            link(cp(qf[0], b))
                        else:
                            link(tt(qf[1], last_, b, ALU.subtract))
                            link(tt(qf[1], qf[1], lf[1], ALU.add))

                    @block.scalar
                    def _(a):
                        a.wait_ge(*dve_done.all())
                        act(qf[d], qf[d], ACT.Exp).then_inc(*act_done.next())

            @block.vector
            def _(v):
                v.wait_ge(*act_done.all())
                v.wait_ge(*pe_done.all())
                tt(kt0, k0, k1, ALU.add).then_inc(*dve_done.next())
                for d in range(2):
                    tt(qf[d], qf[d], q, ALU.mult).then_inc(*dve_done.next())

            @block.tensor
            def _(pe):
                pe.wait_ge(*dve_done.all())
                for T in range(2):
                    for h in range(4):
                        last = mm(b4[T][:, h, :], kt0[:, h, 128 * T:128 * T + 128],
                                  q[:, h, 128 * T:128 * T + 128])
                last.then_inc(*pe_done.next())

            @block.vector
            def _(v):
                v.wait_ge(*pe_done.all())
                for T in range(2):
                    nc.vector.copy_predicated(AT[:, :, T, 128 * T:128 * T + 128],
                                              over(ident, 4).bitcast(I32), b4[T])\
                        .then_inc(*dve_done.next())

            fill(99)
            @block.tensor
            def _(pe):
                pe.wait_ge(*dve_done.all())
                for j in range(4):
                    o = b2[2 + j // 2][:, j % 2, :]
                    for t in range(2):
                        mm(o, Vx[:, t, j * 128:j * 128 + 128], AT[:, j, t, :], start=t == 0, stop=False)
                    for d in range(2):
                        last = mm(o, St[d][:, j, :], qf[d][:, j, :], start=False, stop=d == 1)
                last.then_inc(*pe_done.next())
            mod_of(mod2[:, 16:48, :], 0, 2, bias2(16, 48))
            o, sq, rs = k0, w0_, q0

            @block.scalar
            def _(a):
                a.wait_ge(*pe_done.all())
                for j in range(2):
                    act(o[:, 2 * j:2 * j + 2, :], b2[2 + j], ACT.Copy).then_inc(*act_done.next())
                    act(sq[:, 2 * j:2 * j + 2, :], b2[2 + j], ACT.Square).then_inc(*act_done.next())

            @block.tensor
            def _(pe):
                pe.wait_ge(*act_done.all())
                for j in range(4):
                    last = mm(b2[j // 2][:, j % 2, :], C("ones"), sq[:, j, :])
                last.then_inc(*pe_done.next())
            roots(rs, 0, 1.0 / 128, C("eps")[:, 0:1])

            @block.vector
            def _(v):
                for j in range(4):
                    stt(o[:, j, :], o[:, j, :], col("hg_norm_g_2", j), rs[:, j, :], ALU.mult, ALU.mult)\
                        .then_inc(*dve_done.next())
                v.wait_ge(*dve_done.all())
                link(tt(MIX[:, 2:6, :], o, ZX[:, 22:26, :], ALU.mult))

        load_small()
        for l in range(DEPTH):
            whole = mixing(l)
            if l == 0:
                dense_ffn(D_FF // GROUP)
            else:
                route_top2(whole)
                tap("comb1", comb[:, :, 0:E1])
                skip(PAD_1)
                moe(E1, F1 // GROUP, 128, 1, ALIGN_0 + PAD_1)
            add_output(mods[:, 2 * l + 1, 16:24])
            tap(f"xf{l}", xT[:, :, :])
        second_block()
        return dbg


_SHAPES = {
    "vec": (128, VEC_COLS), "const": (128, CONST_COLS), "late": (128, LATE_COLS),
    "stream": (STREAM_CH, 128, CHUNK_COLS), "x": (128, KD, S), "ctx": (128, KD, S), "pos": (128, S),
}


def arrays_of(i):
    def feature_major(a):
        return np.ascontiguousarray(a.T.reshape(KD, 128, S).transpose(1, 0, 2))
    arrays = {
        "vec": vectors(i), "const": constants(), "late": late_constants(), "stream": stream(i),
        "x": feature_major(i["x"][0]), "ctx": feature_major(i["ctx_2"][0]),
        "pos": np.ascontiguousarray(np.broadcast_to(i["positions"][0][None], (128, S)).astype(np.int32)),
    }
    return {n + "_dram": a for n, a in arrays.items()}


def program(nc, debug=None):
    args = {n: nc.dram_tensor(n + "_dram", s, I32 if n == "pos" else F32, kind="ExternalInput").ap()
            for n, s in _SHAPES.items()}
    out = nc.dram_tensor("out", (S, D), F32, kind="ExternalOutput").ap()
    return build(nc, args["vec"], args["const"], args["late"], args["stream"], args["x"], args["ctx"],
                 args["pos"].bitcast(F32), out, debug)


def kernel(**inputs):
    import concourse.bacc as _bacc
    from concourse.bass_utils import run_bass_kernel_spmd as _run

    arrays = arrays_of({n: np.asarray(a) for n, a in inputs.items()})
    nc = _bacc.Bacc("TRN2", target_bir_lowering=False, num_devices=1)
    program(nc)
    r = _run(nc, [arrays], core_ids=[0])
    return r.results[0]["out"].reshape(1, S, D)
```
